# Optimizing a Trainium2 kernel written in Bass

```python
import math
import jax
import jax.numpy as jnp
from jax import lax
import numpy as np

D_MODEL = 1024
BATCH = 1
SEQ = 512
DEPTH = 1

ATTN_HEADS = 8
ATTN_HEAD_DIM = 64
ATTN_WIDTH = ATTN_HEADS * ATTN_HEAD_DIM
HGRN_HEADS = 8
HGRN_HEAD_DIM = 64
HGRN_WIDTH = HGRN_HEADS * HGRN_HEAD_DIM
MIX_WIDTH = ATTN_WIDTH + HGRN_WIDTH
IN_SIZES = (ATTN_WIDTH, ATTN_WIDTH, ATTN_WIDTH, HGRN_WIDTH, HGRN_WIDTH, HGRN_WIDTH, HGRN_WIDTH)
IN_WIDTH = sum(IN_SIZES)
MOBA_BLOCK = 256
MOBA_TOPK = 3
Q_BLOCK = 64
HGRN_CHUNK = 64
N_BUCKETS = 32
MAX_DISTANCE = 128
N_GROUPS = 4
EXPERTS_PER_GROUP = 4
N_EXPERTS = N_GROUPS * EXPERTS_PER_GROUP
EXPERT_TOPK = 2
D_EXPERT = 512
LN_EPS = 1e-5
RMS_EPS = 1e-6
DEEPNORM_ALPHA = (2.0 * DEPTH) ** 0.25
DEEPNORM_BETA = (8.0 * DEPTH) ** -0.25

kernel_name = 'hybrid_moba_hgrn2_hiermoe_deepnorm'

def layer_norm(x, g, b):
    xf = x.astype(jnp.float32)
    mu = jnp.mean(xf, axis=-1, keepdims=True)
    var = jnp.mean(jnp.square(xf - mu), axis=-1, keepdims=True)
    y = (xf - mu) * lax.rsqrt(var + LN_EPS) * g.astype(jnp.float32) + b.astype(jnp.float32)
    return y.astype(x.dtype)

def t5_bucket(n):
    n = jnp.maximum(n, 0)
    max_exact = N_BUCKETS // 2
    nf = jnp.maximum(n, 1).astype(jnp.float32)
    large = max_exact + (jnp.log(nf / max_exact) / math.log(MAX_DISTANCE / max_exact)
                         * (N_BUCKETS - max_exact)).astype(jnp.int32)
    large = jnp.minimum(large, N_BUCKETS - 1)
    return jnp.where(n < max_exact, n, large)

def moba_attention(q, k, v, bias_table):
    B_, H, S, dh = q.shape
    n_blocks = -(-S // MOBA_BLOCK)
    pad = n_blocks * MOBA_BLOCK - S
    k_pad = jnp.pad(k, ((0, 0), (0, 0), (0, pad), (0, 0)))
    v_pad = jnp.pad(v, ((0, 0), (0, 0), (0, pad), (0, 0)))
    k_blocks = k_pad.reshape(B_, H, n_blocks, MOBA_BLOCK, dh)
    v_blocks = v_pad.reshape(B_, H, n_blocks, MOBA_BLOCK, dh)
    k_mean = jnp.mean(k_blocks.astype(jnp.float32), axis=3)
    n_sel = min(MOBA_TOPK, n_blocks)
    scale = dh ** -0.5
    bias_hb = bias_table.T.astype(jnp.float32)
    bi = jnp.arange(B_)[:, None, None, None]
    hi = jnp.arange(H)[None, :, None, None]
    blk_ids = jnp.arange(n_blocks)
    offs = jnp.arange(MOBA_BLOCK)

    def per_query_block(qb):
        start = qb * Q_BLOCK
        q_c = lax.dynamic_slice_in_dim(q, start, Q_BLOCK, axis=2).astype(jnp.float32)
        q_pos = start + jnp.arange(Q_BLOCK)
        own = start // MOBA_BLOCK
        gate = jnp.einsum('bhqd,bhnd->bhqn', q_c, k_mean)
        gate = jnp.where(blk_ids < own, gate, -jnp.inf)
        _, sel = lax.top_k(gate, n_sel)
        k_sel = k_blocks[bi, hi, sel].astype(jnp.float32)
        v_sel = v_blocks[bi, hi, sel].astype(jnp.float32)
        kpos_sel = sel[..., None] * MOBA_BLOCK + offs
        l_sel = (jnp.einsum('bhqd,bhqjkd->bhqjk', q_c, k_sel) * scale
                 + bias_hb[hi[..., None], t5_bucket(q_pos[:, None, None] - kpos_sel)])
        l_sel = jnp.where((sel < own)[..., None], l_sel, -jnp.inf)
        l_sel = l_sel.reshape(B_, H, Q_BLOCK, n_sel * MOBA_BLOCK)
        k_own = lax.dynamic_slice_in_dim(k_pad, own * MOBA_BLOCK, MOBA_BLOCK, axis=2).astype(jnp.float32)
        v_own = lax.dynamic_slice_in_dim(v_pad, own * MOBA_BLOCK, MOBA_BLOCK, axis=2).astype(jnp.float32)
        rel = q_pos[:, None] - (own * MOBA_BLOCK + offs)[None, :]
        l_own = jnp.einsum('bhqd,bhkd->bhqk', q_c, k_own) * scale + bias_hb[:, t5_bucket(rel)][None]
        l_own = jnp.where(rel >= 0, l_own, -jnp.inf)
        p = jax.nn.softmax(jnp.concatenate([l_sel, l_own], axis=-1), axis=-1)
        p_sel = p[..., :n_sel * MOBA_BLOCK].reshape(B_, H, Q_BLOCK, n_sel, MOBA_BLOCK)
        p_own = p[..., n_sel * MOBA_BLOCK:]
        return (jnp.einsum('bhqjk,bhqjkd->bhqd', p_sel, v_sel)
                + jnp.einsum('bhqk,bhkd->bhqd', p_own, v_own))

    out = lax.map(per_query_block, jnp.arange(S // Q_BLOCK))
    out = out.transpose(1, 2, 0, 3, 4).reshape(B_, H, S, dh)
    return out.astype(q.dtype)

def hgrn2(q, f_logit, i, lb):
    B_, S, H, dk = q.shape
    C = HGRN_CHUNK
    nc = S // C
    f = lb + (1.0 - lb) * jax.nn.sigmoid(f_logit.astype(jnp.float32))
    log_f = jnp.log(f)
    kk = 1.0 - f
    qq = jax.nn.silu(q.astype(jnp.float32))
    vv = i.astype(jnp.float32)

    def chunks(t):
        return t.reshape(B_, nc, C, H, dk).transpose(1, 0, 3, 2, 4)

    causal = jnp.tril(jnp.ones((C, C), dtype=bool))

    def step(state, inp):
        qc, kc, vc, gc = inp
        b = jnp.cumsum(gc, axis=2)
        o_inter = jnp.einsum('bhck,bhkv->bhcv', qc * jnp.exp(b), state)
        diff = b[:, :, :, None, :] - b[:, :, None, :, :]
        decay = jnp.exp(jnp.where(causal[:, :, None], diff, -jnp.inf))
        A = jnp.einsum('bhtk,bhtsk,bhsk->bhts', qc, decay, kc)
        o_intra = jnp.einsum('bhts,bhsv->bhtv', A, vc)
        b_last = b[:, :, -1:, :]
        new_state = (jnp.exp(b_last[:, :, 0, :])[..., None] * state
                     + jnp.einsum('bhsk,bhsv->bhkv', kc * jnp.exp(b_last - b), vc))
        return new_state, o_inter + o_intra

    state0 = jnp.zeros((B_, H, dk, dk), jnp.float32)
    _, o = lax.scan(step, state0, (chunks(qq), chunks(kk), chunks(vv), chunks(log_f)))
    return o.transpose(1, 0, 3, 2, 4).reshape(B_, S, H, dk)

def hier_moe(x, w_group, b_group, w_expert, b_expert, w_gate, w_up, w_down):
    B_, S, D = x.shape
    xt = x.reshape(B_ * S, D)
    g_prob = jax.nn.softmax((xt @ w_group + b_group).astype(jnp.float32), axis=-1)
    g_w, g_idx = lax.top_k(g_prob, 1)
    g_w, g_idx = g_w[:, 0], g_idx[:, 0]
    e_logits_all = jnp.einsum('td,gde->tge', xt, w_expert) + b_expert
    e_logits = jnp.take_along_axis(e_logits_all, g_idx[:, None, None], axis=1)[:, 0]
    e_prob = jax.nn.softmax(e_logits.astype(jnp.float32), axis=-1)
    e_w, e_idx = lax.top_k(e_prob, EXPERT_TOPK)
    e_w = e_w / jnp.sum(e_w, axis=-1, keepdims=True)
    gid = g_idx[:, None] * EXPERTS_PER_GROUP + e_idx
    w_tok = g_w[:, None] * e_w
    combine = jnp.einsum('tk,tke->te', w_tok, jax.nn.one_hot(gid, N_EXPERTS, dtype=jnp.float32)).astype(x.dtype)
    y = jnp.zeros_like(xt)
    for e in range(N_EXPERTS):
        h = jax.nn.silu(xt @ w_gate[e]) * (xt @ w_up[e])
        y = y + combine[:, e:e + 1] * (h @ w_down[e])
    return y.reshape(B_, S, D)

def setup_inputs(seed: int = 0) -> dict:
    key = jax.random.key(seed)
    ks = jax.random.split(key, 20)
    f32 = jnp.float32
    nrm = lambda k, shape: jax.random.normal(k, shape, f32)
    beta = DEEPNORM_BETA
    col_scale = jnp.concatenate([jnp.full((s,), sc, f32) for s, sc in
                                 zip(IN_SIZES, (1.0, 1.0, beta, 1.0, 1.0, beta, 1.0))])
    return {
        'x': nrm(ks[0], (BATCH, SEQ, D_MODEL)),
        'w_in': nrm(ks[1], (DEPTH, D_MODEL, IN_WIDTH)) * D_MODEL ** -0.5 * col_scale,
        't5_bias': nrm(ks[2], (N_BUCKETS, ATTN_HEADS)) * 0.5,
        'hgrn_lb_logits': nrm(ks[3], (DEPTH + 1, HGRN_WIDTH)) * 0.5,
        'hgrn_norm_w': 1.0 + 0.01 * nrm(ks[4], (DEPTH, HGRN_WIDTH)),
        'w_o': nrm(ks[5], (DEPTH, MIX_WIDTH, D_MODEL)) * MIX_WIDTH ** -0.5 * beta,
        'ln1_g': 1.0 + 0.01 * nrm(ks[6], (DEPTH, D_MODEL)),
        'ln1_b': 0.01 * nrm(ks[7], (DEPTH, D_MODEL)),
        'w_group': nrm(ks[8], (DEPTH, D_MODEL, N_GROUPS)) * D_MODEL ** -0.5,
        'b_group': 0.01 * nrm(ks[9], (DEPTH, N_GROUPS)),
        'w_expert': nrm(ks[10], (DEPTH, N_GROUPS, D_MODEL, EXPERTS_PER_GROUP)) * D_MODEL ** -0.5,
        'b_expert': 0.01 * nrm(ks[11], (DEPTH, N_GROUPS, EXPERTS_PER_GROUP)),
        'w_gate': nrm(ks[12], (DEPTH, N_EXPERTS, D_MODEL, D_EXPERT)) * D_MODEL ** -0.5,
        'w_up': nrm(ks[13], (DEPTH, N_EXPERTS, D_MODEL, D_EXPERT)) * D_MODEL ** -0.5,
        'w_down': nrm(ks[14], (DEPTH, N_EXPERTS, D_EXPERT, D_MODEL)) * D_EXPERT ** -0.5 * beta,
        'ln2_g': 1.0 + 0.01 * nrm(ks[15], (DEPTH, D_MODEL)),
        'ln2_b': 0.01 * nrm(ks[16], (DEPTH, D_MODEL)),
    }

def reference(x, w_in, t5_bias, hgrn_lb_logits, hgrn_norm_w, w_o, ln1_g, ln1_b,
              w_group, b_group, w_expert, b_expert, w_gate, w_up, w_down, ln2_g, ln2_b):
    B_, S, D = x.shape
    lb_all = jnp.cumsum(jax.nn.softmax(hgrn_lb_logits.astype(jnp.float32), axis=0), axis=0)
    offsets = np.cumsum((0,) + IN_SIZES)
    for l in range(DEPTH):
        proj = jnp.einsum('bsd,de->bse', x, w_in[l])
        aq, ak, av, hq, hf, hi_, hg = [proj[..., offsets[j]:offsets[j + 1]] for j in range(len(IN_SIZES))]
        to_heads = lambda t: t.reshape(B_, S, ATTN_HEADS, ATTN_HEAD_DIM).transpose(0, 2, 1, 3)
        a = moba_attention(to_heads(aq), to_heads(ak), to_heads(av), t5_bias)
        a = a.transpose(0, 2, 1, 3).reshape(B_, S, ATTN_WIDTH)
        hshape = (B_, S, HGRN_HEADS, HGRN_HEAD_DIM)
        lb = lb_all[l].reshape(HGRN_HEADS, HGRN_HEAD_DIM)
        r = hgrn2(hq.reshape(hshape), hf.reshape(hshape), hi_.reshape(hshape), lb)
        r = r * lax.rsqrt(jnp.mean(jnp.square(r), axis=-1, keepdims=True) + RMS_EPS)
        r = r.reshape(B_, S, HGRN_WIDTH) * hgrn_norm_w[l].astype(jnp.float32)
        r = (r * jax.nn.sigmoid(hg.astype(jnp.float32))).astype(x.dtype)
        mix = jnp.einsum('bse,ed->bsd', jnp.concatenate([a, r], axis=-1), w_o[l])
        x = layer_norm(DEEPNORM_ALPHA * x + mix, ln1_g[l], ln1_b[l])
        moe = hier_moe(x, w_group[l], b_group[l], w_expert[l], b_expert[l], w_gate[l], w_up[l], w_down[l])
        x = layer_norm(DEEPNORM_ALPHA * x + moe, ln2_g[l], ln2_b[l])
    return x


_drawn_inputs = setup_inputs


def setup_inputs(seed=0):
    import zlib

    import numpy as np

    out = dict(_drawn_inputs(seed))
    spreads = {}
    factors = {'t5_bias': 3.17,
     'hgrn_lb_logits': 2.69,
     'hgrn_norm_w': 8.0,
     'ln1_g': 4.435,
     'ln1_b': 4.144,
     'b_group': 8.0,
     'b_expert': 8.0,
     'ln2_g': 5.722,
     'ln2_b': 5.715}
    for name, (base, spread) in spreads.items():
        noise = np.random.default_rng([zlib.crc32(name.encode()), seed]).standard_normal(out[name].shape)
        drawn = base * np.exp(spread * noise) if base else spread * noise
        out[name] = jnp.asarray(drawn.astype(out[name].dtype))
    for name, factor in factors.items():
        out[name] = (out[name] * factor).astype(out[name].dtype)
    return out
```

```python
import math
from contextlib import ExitStack

import numpy as np

import concourse.bass as bass
from concourse import mybir

F32 = mybir.dt.float32
F32R = mybir.dt.float32r
I32 = mybir.dt.int32
U32 = mybir.dt.uint32
ALU = mybir.AluOpType
ACT = mybir.ActivationFunctionType
AX = mybir.AxisListType

P = 128
SEQ, D, WIDTH, HEADS, DH = 512, 1024, 512, 8, 64
T = SEQ // P
KD = D // P
PAIRS = HEADS // 2
CH = 64
NCH = SEQ // CH
N_BUCKETS, MAX_DISTANCE = 32, 128
NG, EPG, NE, DE = 4, 4, 16, 512
NL = NG + NE
LN_EPS, RMS_EPS = 1e-5, 1e-6
ALPHA = 2.0 ** 0.25
SCALE = DH ** -0.5
BIG = 1.0e30
STRIP = SEQ + P
F_FLOOR = 2.0 ** -63
CAP = 128
ROUNDS = SEQ // CAP - 1
PAD_PAIR = 4 * SEQ

UNIT = 2048
RING = 12
WBUF = 3
MIX_RING = 3
BLOCKS = [4, 3, 5, 6, 0, 1, 2]
WIN_UNITS = 2 * len(BLOCKS)
WO_UNITS = 4
MIX_UNITS = WIN_UNITS + WO_UNITS
LEVELS = [32, 16, 8, 4, 2, 1]
GROUPS = 4 * (1 + len(LEVELS))

C_ID, C_TRI, C_ONE = 0, P, 2 * P
C_MASK = 3 * P
C_SCAN = C_MASK + 64 * (1 + len(LEVELS))
C_W4 = C_SCAN + SEQ
C_E16 = C_W4 + 4
C_PAIR = C_E16 + NE
C_PAD = C_PAIR + 4 * T
NC = C_PAD + 2 * NE


def shape_constants():
    c = np.zeros((P, NC), np.float32)
    c[:, C_ID:C_ID + P] = np.eye(P)
    c[:, C_TRI:C_TRI + P] = np.triu(np.ones((P, P)), 1)
    c[:, C_ONE:C_ONE + P] = 1
    s, t = np.arange(P)[:, None] % CH, np.arange(CH)[None, :]
    c[:, C_MASK:C_MASK + 64] = s == t
    for l, m in enumerate(LEVELS):
        c[:, C_MASK + 64 * (l + 1):C_MASK + 64 * (l + 2)] = (s // (2 * m) == t // (2 * m)) & (s % (2 * m) < m) & (t % (2 * m) >= m)
    c[:, C_SCAN:C_SCAN + SEQ] = (np.arange(SEQ) % CH != 0)[None]
    c[:, C_W4:C_W4 + 4] = [4, 3, 2, 1]
    c[:, C_E16:C_E16 + NE] = np.arange(NE)
    for i in range(T):
        tok = i * P + np.arange(P)
        for k in range(2):
            c[:, C_PAIR + 4 * i + 2 * k] = tok
            c[:, C_PAIR + 4 * i + 2 * k + 1] = 2 * tok + k
    c[:, C_PAD + 1::2] = PAD_PAIR
    n = SEQ - 1 - np.arange(STRIP)
    half = N_BUCKETS // 2
    nf = np.maximum(n, 1).astype(np.float32)
    large = half + (np.log(nf / half) / math.log(MAX_DISTANCE / half) * (N_BUCKETS - half)).astype(np.int32)
    bucket = np.where(n < half, np.maximum(n, 0), np.minimum(large, N_BUCKETS - 1))
    hot = np.zeros((N_BUCKETS + 1, STRIP), np.float32)
    hot[bucket, np.arange(STRIP)] = 1
    hot[N_BUCKETS] = n < 0
    return c, hot


def build(nc, t, out, stage):
    with ExitStack() as ctx:
        def sb(name, shape, dt=F32):
            return ctx.enter_context(nc.sbuf_tensor(name, shape, dt))

        def sem(name):
            return ctx.enter_context(nc.semaphore(name))

        def sems(name, n):
            return [sem(f"{name}{i}") for i in range(n)]

        x1_dram = nc.dram_tensor("x1_dram", (SEQ, D), F32).ap()
        pair_dram = nc.dram_tensor("pair_dram", (2 * SEQ, D), F32).ap()
        slot_dram = nc.dram_tensor("slot_dram", (SEQ * NE, 2), I32).ap()
        strip_dram = nc.dram_tensor("strip_dram", (HEADS, STRIP), F32).ap()

        ring = sb("ring", [P, RING, UNIT])
        w_hi = sb("w_hi", [P, WBUF, UNIT], F32R)
        w_lo = sb("w_lo", [P, WBUF, UNIT], F32R)
        act_hi = sb("act_hi", [P, KD, SEQ], F32R)
        act_lo = sb("act_lo", [P, KD, SEQ], F32R)
        misc = sb("misc", [P, 5120])
        cst = sb("cst", [P, NC])
        nw = sb("nw", [P, WIDTH])
        small = sb("small", [P, 512])
        slots = sb("slots", [P, NE, 2], I32)
        ov_rec = sb("ov_rec", [P, 2], I32)
        rec_i = sb("rec_i", [P, T, 2, 2], I32)
        addr_i = sb("addr_i", [P, T, 2], I32)
        over_i = sb("over_i", [P, 1], I32)
        pad_i = sb("pad_i", [P, NE, 2], I32)
        wgt = sb("wgt", [P, T, 2])

        ident = cst[:, C_ID:C_ID + P]
        tri = cst[:, C_TRI:C_TRI + P]
        ones = cst[:, C_ONE:C_ONE + P]

        def flat(slot):
            return ring[:, slot, :]

        x_tok = ring[:, 10:12, :].rearrange("p a (b d) -> p (a b) d", d=D)
        hq = flat(3).rearrange("p (a s) -> p a s", a=PAIRS)
        hk = flat(4).rearrange("p (a s) -> p a s", a=PAIRS)
        hb = flat(5).rearrange("p (a s) -> p a s", a=PAIRS)
        wlev = [flat(7).rearrange("p (a s) -> p a s", a=PAIRS), flat(6).rearrange("p (a s) -> p a s", a=PAIRS)]
        qe = flat(8).rearrange("p (a s) -> p a s", a=PAIRS)
        logf = flat(9).rearrange("p (a s) -> p a s", a=PAIRS)
        ke_tok = flat(9).rearrange("p (i c) -> p i c", i=T)
        amat = flat(10).rearrange("p (g n) -> p g n", g=4)
        hv = flat(11).rearrange("p (i c) -> p i c", i=T)
        mix_r = flat(3).rearrange("p (i c) -> p i c", i=T)
        sq = flat(6)
        state = misc[:, 0:1024].rearrange("p (b a v) -> p b a v", b=2, a=PAIRS)
        gate = misc[:, 1024:3072].rearrange("p (i c) -> p i c", i=T)
        abd = misc[:, 3072:4096].rearrange("p (b i t) -> p b i t", b=2, i=T)
        aq = flat(5).rearrange("p (a s) -> p a s", a=PAIRS)
        ak = flat(6).rearrange("p (a s) -> p a s", a=PAIRS)
        av = flat(7).rearrange("p (i c) -> p i c", i=T)
        strips = ring[:, 8:10, :].rearrange("p a (h n) -> p (a h) n", n=SEQ)
        mix_a = misc[:, 1024:3072].rearrange("p (i c) -> p i c", i=T)
        strip_sb = misc[0:HEADS, 3072:3072 + STRIP]
        x_res = ring[:, 9:11, :].rearrange("p a (b d) -> p (a b) d", d=D)
        lng = flat(11)[:, 0:D]
        lnb = flat(11)[:, D:2 * D]
        x1t = misc[:, 0:2048].rearrange("p (b k t) -> p b k t", b=2, k=KD)
        wr = misc[:, 2048:2048 + KD * NL].rearrange("p (k n) -> p k n", k=KD)
        rt = misc[:, 2304:5120]
        tab = misc[0:N_BUCKETS + 1, 4096:4104]
        hot = misc[0:N_BUCKETS + 1, 4104:4104 + STRIP]

        e_hi = act_hi[:, 0:4, :].rearrange("p (b k) t -> p b (k t)", b=2)
        e_lo = act_lo[:, 0:4, :].rearrange("p (b k) t -> p b (k t)", b=2)
        h_hi, h_lo = act_hi[:, 4, :], act_lo[:, 4, :]
        f_x1 = ring[:, 3:5, :].rearrange("p a (b d) -> p (a b) d", d=D)
        f_g, f_b = flat(5)[:, 0:D], flat(5)[:, D:2 * D]
        xg = misc[:, 0:2048].rearrange("p (b d) -> p b d", b=2)
        gs = misc[:, 2048:2560]
        hh = misc[:, 2560:3072]
        yb = misc[:, 3072:5120].rearrange("p (b d) -> p b d", b=2)

        def o_off(i):
            return P * (i * (i + 1) // 2)

        def p_buf(h, i):
            return flat(10 + h % 2)[:, o_off(i):o_off(i) + P * (i + 1)]

        def pt_buf(h, i):
            if h % 2 == 0:
                return flat(4)[:, o_off(i):o_off(i) + P * (i + 1)]
            if i < 3:
                return flat(10)[:, 1280 + o_off(i):1280 + o_off(i) + P * (i + 1)]
            return flat(4)[:, 1280:1280 + P * (i + 1)]

        def f_pair(i):
            return flat(6 + i)

        lb2 = small[:, 0:8].rearrange("p (r a) -> p r a", r=2)
        lbm = small[:, 8:12]
        lbe = small[:, 12:20].rearrange("p (r a) -> p r a", r=2)
        lbs = small[:, 20:24]
        lb = small[:, 24:28]
        oml = small[:, 28:32]
        noml = small[:, 32:36]
        flast = small[:, 40:72].rearrange("p (a c) -> p a c", a=PAIRS)
        ms = small[:, 72:104]
        rs = small[:, 104:136]
        nmax = small[:, 136:168]
        psums = small[:, 168:200]
        prec = small[:, 200:232]
        bst = small[:, 232:280].rearrange("p (i b n) -> p i b n", i=T, b=2)
        mv = small[:, 280:288].rearrange("p (i n) -> p i n", i=T)
        rstd = small[:, 288:292]
        nmr = small[:, 292:296]
        eps_ln = small[:, 296:297]
        eps_rms = small[:, 297:298]
        rbias = small[:, 300:320]

        r_at = [0]

        def rcol(*shape):
            n = int(np.prod(shape))
            v = rt[:, T * NE + r_at[0]:T * NE + r_at[0] + n]
            r_at[0] += n
            names = "abcd"[:len(shape)]
            return v.rearrange("p (%s) -> p %s" % (" ".join(names), " ".join(names)), **dict(zip(names, shape)))

        r_msk = rt[:, 0:T * NE].rearrange("p (i e) -> p i e", i=T)
        r_l, r_m, r_g, r_gh, r_e, r_tmp = rcol(T, NL), rcol(T, 1), rcol(T, NG), rcol(T, NG), rcol(T, EPG), rcol(T, EPG)
        r_gsum, r_gw, r_top, r_top2 = rcol(T, 1), rcol(T, 1), rcol(T, 1), rcol(T, 1)
        r_h, r_sel, r_pos, r_t16, r_adr, r_cnt = rcol(2, T, EPG), rcol(2, T, NE), rcol(T, NE), rcol(T, NE), rcol(T, 2), rcol(1)
        r_ge, r_ee = r_g, r_e

        psum = ctx.enter_context(nc.psum_tensor("psum", [P, 8, 512], F32))

        s_const, s_x, s_lb, s_small = sem("s_const"), sem("s_x"), sem("s_lb"), sem("s_small")
        s_raw = sems("s_raw", RING)
        s_hi, s_lo, s_used = sem("s_hi"), sem("s_lo"), sem("s_used")
        s_xt, s_xthi, s_xtlo = sem("s_xt"), sem("s_xthi"), sem("s_xtlo")
        s_evac = sem("s_evac")
        s_dve, s_act, s_pool = sem("s_dve"), sem("s_act"), sem("s_pool")
        s_lbready, s_lnf, s_kk, s_scan = sem("s_lbready"), sem("s_lnf"), sem("s_kk"), sem("s_scan")
        s_eb, s_d, s_ed, s_qe, s_ke = sem("s_eb"), sem("s_d"), sem("s_ed"), sem("s_qe"), sem("s_ke")
        s_w, s_zero = sem("s_w"), sem("s_zero")
        s_ket, s_ketok, s_kv, s_state = sem("s_ket"), sem("s_ketok"), sem("s_kv"), sem("s_state")
        s_prod, s_copied, s_abd, s_av = sem("s_prod"), sem("s_copied"), sem("s_abd"), sem("s_av")
        s_sq, s_ms, s_sqrt, s_r, s_gate = sem("s_sq"), sem("s_ms"), sem("s_sqrt"), sem("s_r"), sem("s_gate")
        s_tab, s_strip, s_stripsb, s_stripd, s_strips = sem("s_tab"), sem("s_strip"), sem("s_stripsb"), sem("s_stripd"), sem("s_strips")
        s_score, s_logit, s_prob, s_pt, s_ptsb, s_pv, s_mixa = sem("s_score"), sem("s_logit"), sem("s_prob"), sem("s_pt"), sem("s_ptsb"), sem("s_pv"), sem("s_mixa")
        s_mixt, s_mixthi, s_mixtlo = sem("s_mixt"), sem("s_mixthi"), sem("s_mixtlo")
        s_wo, s_xres, s_ln, s_lnw, s_var, s_std, s_x1 = sem("s_wo"), sem("s_xres"), sem("s_ln"), sem("s_lnw"), sem("s_var"), sem("s_std"), sem("s_x1")
        s_x1out, s_x1t, s_x1tsb, s_logits, s_wr = sem("s_x1out"), sem("s_x1t"), sem("s_x1tsb"), sem("s_logits"), sem("s_wr")
        s_abdfree, s_inter, s_mixr, s_flag = sem("s_abdfree"), sem("s_inter"), sem("s_mixr"), sem("s_flag")
        s_lin, s_rexp, s_mask, s_pos, s_addr = sem("s_lin"), sem("s_rexp"), sem("s_mask"), sem("s_pos"), sem("s_addr")
        s_pads, s_slotw, s_slots = sem("s_pads"), sem("s_slotw"), sem("s_slots")
        s_out, s_eps, s_x1n, s_rneed, s_memz, s_half = sem("s_out"), sem("s_eps"), sem("s_x1n"), sem("s_rneed"), sem("s_memz"), sem("s_half")
        s_gidx, s_sidx, s_st1, s_st2, s_bn, s_lg, s_res = sem("s_gidx"), sem("s_sidx"), sem("s_st1"), sem("s_st2"), sem("s_bn"), sem("s_lg"), sem("s_res")
        s_fw, s_facc, s_fl, s_fn, s_fm = sem("s_fw"), sem("s_facc"), sem("s_fl"), sem("s_fn"), sem("s_fm")
        s_xg = sems("s_xg", 2)
        s_et, s_ethi, s_etlo = sem("s_et"), sem("s_ethi"), sem("s_etlo")
        s_silu, s_h, s_ht, s_hthi, s_htlo = sem("s_silu"), sem("s_h"), sem("s_ht"), sem("s_hthi"), sem("s_htlo")
        s_y = sem("s_y")
        s_yout = sems("s_yout", 2)
        s_ov = {n: sem(f"s_ov_{n}") for n in ("turn", "free", "idx", "w", "xg", "xt", "xtsb", "gu", "silu", "h", "ht", "htsb", "y", "ysb", "yout")}
        s_pairs = sems("s_pairs", T)
        s_xo, s_fin, s_fv, s_fs, s_ft = sem("s_xo"), sem("s_fin"), sem("s_fv"), sem("s_fs"), sem("s_ft")

        w_in = t["w_in"].rearrange("(p k) (b n) -> p k b n", p=P, n=WIDTH)
        w_o = t["w_o"].rearrange("(k p) d -> p k d", p=P)
        wg = t["w_gate"].rearrange("e (p k) f -> e p (k f)", p=P)
        wu = t["w_up"].rearrange("e (p k) f -> e p (k f)", p=P)
        wd = t["w_down"].rearrange("e (p c) d -> e p (c d)", p=P)

        def bank(b, n=512):
            return psum[:, b, 0:n]

        def banks(b, n):
            return psum[:, b:b + n, :].rearrange("p b n -> p (b n)")

        def turned(ap):
            return ap.rearrange("p (n q) -> p n q", q=P)[:, :, ::-1]

        block = ctx.enter_context(nc.Block())

        @block.sync
        def _(sp):
            sp.dma_start(x_tok, t["x"].rearrange("(i p) d -> p i d", p=P)).then_inc(s_x, 16)
            sp.dma_start(cst[:, :], t["c_main"]).then_inc(s_const, 16)

            def mixer_unit(u):
                if u >= MIX_RING:
                    sp.wait_ge(s_lo, u - MIX_RING + 1)
                dst = ring[:, u % MIX_RING, :]
                if u < WIN_UNITS:
                    k = 4 * (u % 2)
                    sp.dma_start(dst.rearrange("p (k n) -> p k n", k=4), w_in[:, k:k + 4, BLOCKS[u // 2], :]).then_inc(s_raw[u % MIX_RING], 16)
                else:
                    k = 2 * (u - WIN_UNITS)
                    sp.dma_start(dst.rearrange("p (k n) -> p k n", k=2), w_o[:, k:k + 2, :]).then_inc(s_raw[u % MIX_RING], 16)

            for u in range(3):
                mixer_unit(u)
            with nc.allow_non_contiguous_dma(reason="a few small parameters"):
                sp.dma_start(lb2, t["hgrn_lb_logits"].rearrange("r (a p) -> p r a", p=P)).then_inc(s_lb, 16)
            sp.dma_start(tab[0:N_BUCKETS, :], t["t5_bias"]).then_inc(s_tab, 16)
            sp.dma_start(rbias[:, 0:NG], t["b_group"].broadcast_to((P, NG))).then_inc(s_small, 16)
            sp.dma_start(rbias[:, NG:NL], t["b_expert"].broadcast_to((P, NE))).then_inc(s_small, 16)
            sp.dma_start(hot, t["c_hot"]).then_inc(s_tab, 16)
            sp.dma_start(nw[:, :], t["hgrn_norm_w"].broadcast_to((P, WIDTH))).then_inc(s_small, 16)
            for u in range(3, 6):
                mixer_unit(u)
            sp.wait_ge(s_stripsb, 2)
            sp.dma_start(strip_dram, strip_sb).then_inc(s_stripd, 16)
            for u in range(6, 14):
                mixer_unit(u)
            sp.wait_ge(s_av, T)
            sp.wait_ge(s_stripd, 16)
            for h in range(HEADS):
                skew = bass.AP(tensor=strip_dram.tensor, offset=h * STRIP, ap=[[1, P], [1, SEQ]])
                sp.dma_start(strips[:, h, :], skew).then_inc(s_strips, 16)
            for u in range(14, MIX_UNITS):
                mixer_unit(u)

            def expert_unit(m, e_g, e_d, slot):
                kind, half = m
                src, e = {"g": (wg, e_g), "u": (wu, e_g), "d": (wd, e_d)}[kind]
                sp.dma_start(ring[:, slot, :], src[bass.ds(e, 1), :, half * UNIT:(half + 1) * UNIT].rearrange("a p n -> (a p) n")).then_inc(s_raw[slot], 16)

            sp.wait_ge(s_mixtlo, KD)
            sp.dma_start(x_res, t["x"].rearrange("(i p) d -> p i d", p=P)).then_inc(s_xres, 16)
            sp.dma_start(lng, t["ln1_g"].broadcast_to((P, D))).then_inc(s_lnw, 16)
            sp.dma_start(lnb, t["ln1_b"].broadcast_to((P, D))).then_inc(s_lnw, 16)
            sp.dma_start(wr[:, :, 0:NG], t["w_group"].rearrange("(p k) g -> p k g", p=P)).then_inc(s_wr, 16)
            for g in range(NG):
                sp.dma_start(wr[:, :, NG + EPG * g:NG + EPG * (g + 1)],
                             t["w_expert"][g].rearrange("(p k) e -> p k e", p=P)).then_inc(s_wr, 16)
            order = [("g", 0), ("g", 1), ("u", 0), ("u", 1)]
            step = [("g", 0), ("g", 1), ("d", 0), ("d", 1), ("u", 0), ("u", 1)]
            for n, m in enumerate(order + step[:2]):
                expert_unit(m, n // 4, 0, (n + 3) % RING)
            for i in range(T):
                sp.wait_ge(s_x1, i + 1)
                sp.dma_start(x1_dram[i * P:(i + 1) * P, :], x_res[:, i, :]).then_inc(s_x1out, 16)
            if stage == "x1":
                for i in range(T):
                    sp.dma_start(out[i * P:(i + 1) * P, :], x_res[:, i, :]).then_inc(s_out, 16)
                sp.wait_ge(s_out, 16 * T)
            sp.wait_ge(s_x1out, 16 * T)
            sp.wait_ge(s_x1t, T)
            for n in (6, 7, 8):
                expert_unit(step[n - 4], 1, 0, n + 3)
            sp.wait_ge(s_slotw, 16 * 2 * T)
            sp.dma_start(slots[:, :, :], slot_dram[0:CAP * NE, :].rearrange("(p e) r -> p e r", e=NE)).then_inc(s_slots, 16)
            sp.wait_ge(s_lo, 16)
            expert_unit(step[5], 1, 0, 0)
            for n in (10, 11):
                sp.wait_ge(s_lo, n + 7)
                expert_unit(step[n - 10], 2, 1, (n + 3) % RING)
            with sp.Fori(0, NE // 2 - 2) as j:
                for q in range(12):
                    n = 12 + q
                    sp.wait_ge(s_lo, n + 7 + 12 * j)
                    kind = step[(n - 4) % 6]
                    s = 1 + (n - 4) // 6
                    expert_unit(kind, s + 2 * j, s - 1 + 2 * j, (n + 3) % RING)
            for n in range(12 + 12 * (NE // 2 - 2), 6 * NE):
                s = 1 + (n - 4) // 6
                kind = step[(n - 4) % 6]
                if s == NE:
                    kind = [("d", 0), ("d", 1)][n - (4 + 6 * (NE - 1))]
                sp.wait_ge(s_lo, n + 7)
                expert_unit(kind, s, s - 1, (n + 3) % RING)

            sp.wait_ge(s_flag, 2)
            over = sp.value_load(over_i[0:1, 0:1], min_val=0, max_val=1)
            with sp.If(over > 0):
                for b in range(2):
                    sp.wait_ge(s_yout[b], 16 * (NE // 2))
                ov_slots = slot_dram.rearrange("(r p e) c -> r e p c", p=P, e=NE)
                with sp.Fori(0, ROUNDS) as r:
                    with sp.Fori(0, NE) as e:
                        sp.wait_ge(s_ov["free"], r * NE + e + 1)
                        sp.dma_start(ov_rec[:, :], ov_slots[bass.ds(r + 1, 1), bass.ds(e, 1), :, :].rearrange("a b p c -> (a b p) c")).then_inc(s_ov["idx"], 16)
                        for q in range(6):
                            sp.dma_start(ring[:, q, :], (wg, wu, wd)[q // 2][bass.ds(e, 1), :, (q % 2) * UNIT:(q % 2 + 1) * UNIT].rearrange("a p n -> (a p) n")).then_inc(s_ov["w"], 16)
                sp.wait_ge(s_ov["yout"], 16 * ROUNDS * NE)

            sp.wait_ge(s_lo, MIX_UNITS + 6 * NE)
            sp.dma_start(f_x1, x1_dram.rearrange("(i p) d -> p i d", p=P)).then_inc(s_xo, 16)
            sp.dma_start(f_g, t["ln2_g"].broadcast_to((P, D))).then_inc(s_fw, 16)
            sp.dma_start(f_b, t["ln2_b"].broadcast_to((P, D))).then_inc(s_fw, 16)
            for b in range(2):
                sp.wait_ge(s_yout[b], 16 * (NE // 2))
            for i in range(T):
                sp.dma_start(f_pair(i), pair_dram[i * 2 * P:(i + 1) * 2 * P, :].rearrange("(p k) d -> p (k d)", k=2)).then_inc(s_pairs[i], 16)
            for i in range(T):
                sp.wait_ge(s_fin, i + 1)
                sp.dma_start(out[i * P:(i + 1) * P, :], f_x1[:, i, :]).then_inc(s_out, 16)
            sp.wait_ge(s_out, 16 * T)

        @block.gpsimd
        def _(pool):
            pool.wait_ge(s_small, 16 * 3)
            pool.wait_ge(s_scan, PAIRS)
            b_ch = hb.rearrange("p a (c s) -> p (a c) s", s=CH)
            pool.tensor_tensor(wlev[1].rearrange("p a (c s) -> p (a c) s", s=CH), b_ch,
                               b_ch[:, :, CH - 1:CH].broadcast_to((P, PAIRS * NCH, CH)), ALU.subtract).then_inc(s_d, 1)
            for l, m in enumerate(LEVELS):
                if l == 0:
                    pass
                elif l == 1:
                    pool.wait_ge(s_ket, T)
                else:
                    pool.wait_ge(s_prod, 4 * (l - 1) + 4)
                src = hb.rearrange("p a (n s) -> p (a n) s", s=2 * m)
                pool.tensor_tensor(wlev[l % 2].rearrange("p a (n s) -> p (a n) s", s=2 * m), src,
                                   src[:, :, m - 1:m].broadcast_to((P, SEQ * PAIRS // (2 * m), 2 * m)),
                                   ALU.subtract).then_inc(s_d, 1)
                if l == 1:
                    pool.wait_ge(s_evac, 4)
                    for i in range(T):
                        pool.tensor_tensor(gate[:, i, :], gate[:, i, :], nw[:, :], ALU.mult).then_inc(s_gate, 1)
            pool.wait_ge(s_const, 16)
            pool.tensor_copy(pad_i[:, :, :].rearrange("p e r -> p (e r)"), cst[:, C_PAD:C_PAD + 2 * NE]).then_inc(s_pool, 1)
            pool.tensor_copy(rec_i[:, :, :, :].rearrange("p i k r -> p (i k r)"), cst[:, C_PAIR:C_PAIR + 4 * T]).then_inc(s_pool, 1)
            pool.wait_ge(s_pool, 2)
            for r in range(SEQ // P):
                pool.dma_start(slot_dram[r * P * NE:(r + 1) * P * NE, :].rearrange("(p e) r -> p e r", e=NE),
                               pad_i[:, :, :]).then_inc(s_pads, 16)
            pool.wait_ge(s_pads, 16 * (SEQ // P))
            pool.wait_ge(s_addr, 1)
            for i in range(T):
                for k in range(2):
                    pool.indirect_dma_start(out=slot_dram, out_offset=bass.IndirectOffsetOnAxis(ap=addr_i[:, i, k:k + 1].bitcast(U32), axis=0),
                                            in_=rec_i[:, i, k, :], in_offset=None).then_inc(s_slotw, 16)
            pool.wait_ge(s_slots, 16)
            pool.wait_ge(s_x1out, 16 * T)

            def gather(e):
                if e >= 2:
                    pool.wait_ge(s_et, e - 1)
                pool.indirect_dma_start(out=xg[:, e % 2, :], out_offset=None, in_=x1_dram,
                                        in_offset=bass.IndirectOffsetOnAxis(ap=slots[:, e, 0:1].bitcast(U32), axis=0)).then_inc(s_xg[e % 2], 16)

            gather(0)
            gather(1)
            for e in range(NE):
                if e + 2 < NE:
                    gather(e + 2)
                pool.wait_ge(s_y, e + 1)
                pool.indirect_dma_start(out=pair_dram, out_offset=bass.IndirectOffsetOnAxis(ap=slots[:, e, 1:2].bitcast(U32), axis=0),
                                        in_=yb[:, e % 2, :], in_offset=None, bounds_check=2 * SEQ - 1, oob_is_err=False).then_inc(s_yout[e % 2], 16)
            for b in range(2):
                pool.wait_ge(s_yout[b], 16 * (NE // 2))

            pool.wait_ge(s_flag, 2)
            over = pool.value_load(over_i[0:1, 0:1], min_val=0, max_val=1)
            with pool.If(over > 0):
                pool.sem_inc(s_ov["free"], 1)
                with pool.Fori(0, ROUNDS * NE) as i:
                    pool.wait_ge(s_ov["idx"], 16 * i + 16)
                    pool.sem_inc(s_ov["turn"], 1)
                    pool.indirect_dma_start(out=xg[:, 0, :], out_offset=None, in_=x1_dram,
                                            in_offset=bass.IndirectOffsetOnAxis(ap=ov_rec[:, 0:1].bitcast(U32), axis=0)).then_inc(s_ov["xg"], 16)
                    pool.wait_ge(s_ov["ysb"], i + 1)
                    pool.sem_inc(s_ov["turn"], 1)
                    pool.indirect_dma_start(out=pair_dram, out_offset=bass.IndirectOffsetOnAxis(ap=ov_rec[:, 1:2].bitcast(U32), axis=0),
                                            in_=yb[:, 0, :], in_offset=None, bounds_check=2 * SEQ - 1, oob_is_err=False).then_inc(s_ov["yout"], 16)
                    pool.wait_ge(s_ov["yout"], 16 * i + 16)
                    pool.sem_inc(s_ov["free"], 1)

            for i in range(T):
                pool.wait_ge(s_fm, i + 1)
                pool.tensor_tensor(f_x1[:, i, :], f_x1[:, i, :], f_b, ALU.add).then_inc(s_fin, 1)

        @block.tensor
        def _(pe):
            def three(dst, lh, ll, rh, rl, first, last, done=None):
                pe.matmul(dst, lh, rh, start=first, stop=False, skip_group_check=True)
                pe.matmul(dst, lh, rl, start=False, stop=False, skip_group_check=True)
                return pe.matmul(dst, ll, rh, start=False, stop=last, skip_group_check=True)

            pe.wait_ge(s_x, 16)
            pe.wait_ge(s_const, 16)
            for k in range(KD):
                for i in range(T):
                    last = pe.transpose(psum[:, k, i * P:(i + 1) * P], x_tok[:, i, k::KD], ident)
                last.then_inc(s_xt, 1)

            def project(n):
                base = 4 * (n % 2)
                by_channel = BLOCKS[n] in (0, 1, 3, 4)
                for u in (2 * n, 2 * n + 1):
                    pe.wait_ge(s_lo, u + 1)
                    w = u % WBUF
                    for kk in range(4):
                        k = 4 * (u % 2) + kk
                        if n == 0:
                            pe.wait_ge(s_xtlo, max(k + 1, 4))
                        for j in range(4):
                            ws = slice(kk * WIDTH + j * P, kk * WIDTH + (j + 1) * P)
                            wr_ = slice(kk * WIDTH, (kk + 1) * WIDTH)
                            ts = slice(j * P, (j + 1) * P)
                            first, last = k == 0, k == KD - 1
                            if by_channel:
                                ins = three(bank(base + j), w_hi[:, w, ws], w_lo[:, w, ws], act_hi[:, k, :], act_lo[:, k, :], first, last)
                            else:
                                ins = three(bank(base + j), act_hi[:, k, ts], act_lo[:, k, ts], w_hi[:, w, wr_], w_lo[:, w, wr_], first, last)
                    ins.then_inc(s_used, 1)

            for n in range(4):
                if n == 1:
                    pe.wait_ge(s_xtlo, KD)
                if n >= 2:
                    pe.wait_ge(s_evac, n - 1)
                if n == 1:
                    pe.wait_ge(s_tab, 32)
                    pe.wait_ge(s_flag, 1)
                    pe.matmul(psum[0:HEADS, 7, 0:512], tab, hot[:, 0:512], start=True, stop=True).then_inc(s_strip, 1)
                    pe.matmul(psum[0:HEADS, 6, 0:P], tab, hot[:, 512:STRIP], start=True, stop=True).then_inc(s_strip, 1)
                    pe.wait_ge(s_stripsb, 2)
                project(n)

            pe.wait_ge(s_ke, 1)
            pe.wait_ge(s_evac, 3)
            for i in range(T):
                if i >= 2:
                    pe.wait_ge(s_ketok, i - 1)
                for a in range(PAIRS):
                    last = pe.transpose(psum[:, 2 + i % 2, a * P:(a + 1) * P], wlev[1][:, a, i * P:(i + 1) * P], ident)
                last.then_inc(s_ket, 1)

            def products(g):
                lev, q = g // 4, g % 4
                pg, par = q // 2, q % 2
                rows = slice(64 * par, 64 * par + 64)
                if g >= 2:
                    pe.wait_ge(s_copied, g - 1)
                for hh2 in range(2):
                    a = 2 * pg + hh2
                    for c in range(NCH):
                        cs = slice(c * CH, (c + 1) * CH)
                        if lev == 0:
                            lhs, rhs = hk[rows, a, cs], hq[rows, a, cs]
                        else:
                            lhs = rhs = wlev[(lev - 1) % 2][rows, a, cs]
                        o = psum[64 * (c % 2):64 * (c % 2) + 64, g % 2, hh2 * 256 + (c // 2) * CH:hh2 * 256 + (c // 2 + 1) * CH]
                        last = pe.matmul(o, lhs, rhs, start=(hh2 == 0 and c < 2), stop=True, skip_group_check=True)
                last.then_inc(s_prod, 1)

            pe.wait_ge(s_evac, 4)
            pe.wait_ge(s_qe, 1)
            pe.wait_ge(s_zero, 1)
            for c in range(NCH):
                rows = slice(64 * (c % 2), 64 * (c % 2) + 64)
                if c < NCH - 1:
                    if c == 0:
                        pe.wait_ge(s_ketok, T)
                    if c >= 2:
                        pe.wait_ge(s_state, c - 1)
                    for a in range(PAIRS):
                        last = pe.matmul(psum[:, 2 + c % 2, a * P:(a + 1) * P], ke_tok[rows, c // 2, a * P:(a + 1) * P],
                                         hv[rows, c // 2, a * P:(a + 1) * P], start=(a == 0), stop=True, skip_group_check=True)
                    last.then_inc(s_kv, 1)
                if c == 4:
                    pe.wait_ge(s_w, 1)
                products(c)
                if c >= 1:
                    pe.wait_ge(s_state, c)
                for a in range(PAIRS):
                    last = pe.matmul(psum[rows, 4 + c // 2, a * P:(a + 1) * P], qe[:, a, c * CH:(c + 1) * CH],
                                     state[:, c % 2, a, :], start=(a == 0), stop=False, skip_group_check=True)
                last.then_inc(s_inter, 1)
            for g in range(8, GROUPS):
                if g % 4 == 0:
                    pe.wait_ge(s_w, g // 4)
                products(g)
            for h in range(HEADS):
                pe.wait_ge(s_abd, h + 1)
                for i in range(T):
                    last = pe.matmul(psum[:, 4 + i, h * DH:(h + 1) * DH], abd[:, h % 2, i, :], hv[:, i, h * DH:(h + 1) * DH],
                                     start=False, stop=(h == HEADS - 1), skip_group_check=True)
                    if h == HEADS - 1:
                        last.then_inc(s_av, 1)
                if h < HEADS - 1:
                    last.then_inc(s_abdfree, 1)

            pe.wait_ge(s_copied, GROUPS)
            project(4)
            pe.wait_ge(s_r, T)
            project(5)
            pe.wait_ge(s_evac, 5)
            project(6)
            pe.wait_ge(s_evac, 7)
            NU = HEADS * T

            def scores(n):
                h, i = n // T, n % T
                rows = slice(64 * (h % 2), 64 * (h % 2) + 64)
                if n >= 2:
                    pe.wait_ge(s_logit, n - 1)
                pe.matmul(psum[:, 4 + n % 2, 0:P * (i + 1)], aq[rows, h // 2, i * P:(i + 1) * P], ak[rows, h // 2, 0:P * (i + 1)],
                          start=True, stop=True).then_inc(s_score, 1)

            def probs_t(n):
                h, i = n // T, n % T
                pe.wait_ge(s_prob, n + 1)
                if n >= 2:
                    pe.wait_ge(s_ptsb, n - 1)
                for j in range(i + 1):
                    last = pe.transpose(psum[:, 6 + n % 2, j * P:(j + 1) * P], p_buf(h, i)[:, j * P:(j + 1) * P], ident)
                last.then_inc(s_pt, 1)

            def values(n):
                h, i = n // T, n % T
                pe.wait_ge(s_ptsb, n + 1)
                for j in range(i + 1):
                    last = pe.matmul(psum[:, i, h * DH:(h + 1) * DH], pt_buf(h, i)[:, j * P:(j + 1) * P], av[:, j, h * DH:(h + 1) * DH],
                                     start=(j == 0), stop=(j == i), skip_group_check=True)
                last.then_inc(s_pv, 1)

            for n in range(NU + 3):
                if n < NU:
                    scores(n)
                if 0 <= n - 2 < NU:
                    probs_t(n - 2)
                if 0 <= n - 3 < NU:
                    values(n - 3)
            for n in range(KD):
                k = (4 + n) % KD
                src = mix_r if k >= 4 else mix_a
                if n >= 4:
                    pe.wait_ge(s_mixtlo, n - 3)
                else:
                    pe.wait_ge(s_mixr, T)
                    pe.wait_ge(s_ptsb, NU)
                if n == 4:
                    pe.wait_ge(s_mixa, T)
                for i in range(T):
                    last = pe.transpose(psum[:, 4 + n % 4, i * P:(i + 1) * P], src[:, i, (k % 4) * P:(k % 4 + 1) * P], ident)
                last.then_inc(s_mixt, 1)
            pe.wait_ge(s_mixtlo, KD)
            for q in range(WO_UNITS):
                u = WIN_UNITS + q
                pe.wait_ge(s_lo, u + 1)
                w = u % WBUF
                for i in range(T):
                    ts = slice(i * P, (i + 1) * P)
                    for half in range(2):
                        for kk in range(2):
                            k = 2 * q + kk
                            ws = slice(kk * D + half * 512, kk * D + half * 512 + 512)
                            ins = three(bank(2 * i + half), act_hi[:, k, ts], act_lo[:, k, ts], w_hi[:, w, ws], w_lo[:, w, ws],
                                        k == 0, k == KD - 1)
                    if q == WO_UNITS - 1 and i < T - 1:
                        ins.then_inc(s_wo, 1)
                ins.then_inc(s_used, 1)
            pe.wait_ge(s_wr, 16 * 5)
            for i in range(T):
                pe.wait_ge(s_x1, i + 1)
                for k in range(KD):
                    last = pe.transpose(psum[:, 2 * i + k // 4, (k % 4) * P:(k % 4 + 1) * P], x_res[:, i, k::KD], ident)
                last.then_inc(s_x1t, 1)
                pe.wait_ge(s_x1tsb, i + 1)
                for k in range(KD):
                    last = pe.matmul(psum[:, 2 * i, 0:NL], x1t[:, i % 2, k, :], wr[:, k, :], start=(k == 0), stop=(k == KD - 1))
                last.then_inc(s_logits, 1)
            msk = rt[:, 0:T * NE].rearrange("p (i e) -> p i e", i=T)
            pe.wait_ge(s_mask, 1)
            for i in range(T + 1):
                for i2 in range(min(i + 1, T)):
                    last = pe.matmul(psum[:, 7, i * NE:(i + 1) * NE], tri if i2 == i else ones, msk[:, i2, :],
                                     start=(i2 == 0), stop=(i2 == min(i, T - 1)), skip_group_check=True)
            last.then_inc(s_pos, 1)
            if stage == "x1":
                return

            def transpose_x(e, b):
                pe.wait_ge(s_xg[b], 8 * (e - b) + 16)
                if not (isinstance(e, int) and e == 0):
                    pe.wait_ge(s_etlo, e)
                for k in range(KD):
                    last = pe.transpose(psum[:, k // 4, (k % 4) * P:(k % 4 + 1) * P], xg[:, b, k::KD], ident)
                last.then_inc(s_et, 1)

            def in_unit(dst, b, half, v0, j):
                pe.wait_ge(s_lo, MIX_UNITS + v0 + 1 + 12 * j)
                w = v0 % WBUF
                for kk in range(4):
                    k = 4 * half + kk
                    xs = slice(k * P, (k + 1) * P)
                    ws = slice(kk * DE, (kk + 1) * DE)
                    last = three(bank(dst), e_hi[:, b, xs], e_lo[:, b, xs], w_hi[:, w, ws], w_lo[:, w, ws], k == 0, k == KD - 1)
                last.then_inc(s_used, 1)

            def transpose_h(s):
                pe.wait_ge(s_h, s)
                for c in range(4):
                    last = pe.transpose(psum[:, 4, c * P:(c + 1) * P], hh[:, c::4], ident)
                last.then_inc(s_ht, 1)

            def down_unit(half, v0, j):
                pe.wait_ge(s_lo, MIX_UNITS + v0 + 1 + 12 * j)
                w = v0 % WBUF
                for cc in range(2):
                    c = 2 * half + cc
                    hs = slice(c * P, (c + 1) * P)
                    for dhalf in range(2):
                        ws = slice(cc * D + dhalf * 512, cc * D + dhalf * 512 + 512)
                        last = three(bank(5 + dhalf), h_hi[:, hs], h_lo[:, hs], w_hi[:, w, ws], w_lo[:, w, ws], c == 0, c == 3)
                last.then_inc(s_used, 1)

            def step(s0, j, following=True):
                s, b, v = s0 + 2 * j, s0 % 2, 4 + 6 * (s0 - 1)
                pe.wait_ge(s_etlo, s + 1)
                pe.wait_ge(s_silu, s)
                in_unit(2, b, 0, v, j)
                transpose_h(s)
                in_unit(2, b, 1, v + 1, j)
                pe.wait_ge(s_htlo, s)
                if s0 > 1:
                    pe.wait_ge(s_y, s - 1)
                down_unit(0, v + 2, j)
                down_unit(1, v + 3, j)
                if following:
                    transpose_x(s + 1, 1 - b)
                in_unit(3, b, 0, v + 4, j)
                in_unit(3, b, 1, v + 5, j)

            transpose_x(0, 0)
            pe.wait_ge(s_etlo, 1)
            in_unit(2, 0, 0, 0, 0)
            in_unit(2, 0, 1, 1, 0)
            transpose_x(1, 1)
            in_unit(3, 0, 0, 2, 0)
            in_unit(3, 0, 1, 3, 0)
            step(1, 0)
            with pe.Fori(0, NE // 2 - 2) as j:
                step(2, j)
                step(3, j)
            step(NE - 2, 0)
            step(NE - 1, 0, following=False)
            transpose_h(NE)
            pe.wait_ge(s_htlo, NE)
            pe.wait_ge(s_y, NE - 1)
            down_unit(0, 6 * NE - 2, 0)
            down_unit(1, 6 * NE - 1, 0)

            pe.wait_ge(s_flag, 2)
            over = pe.value_load(over_i[0:1, 0:1], min_val=0, max_val=1)
            with pe.If(over > 0):
                pe.wait_ge(s_y, NE)
                with pe.Fori(0, ROUNDS * NE) as i:
                    pe.wait_ge(s_ov["xg"], 16 * i + 16)
                    for k in range(KD):
                        last = pe.transpose(psum[:, k // 4, (k % 4) * P:(k % 4 + 1) * P], xg[:, 0, k::KD], ident)
                    last.then_inc(s_ov["xt"], 1)
                    pe.wait_ge(s_ov["xtsb"], i + 1)
                    pe.wait_ge(s_ov["w"], 16 * 6 * i + 16 * 6)
                    for which in range(2):
                        for k in range(KD):
                            last = pe.matmul(bank(2 + which), flat(6)[:, k * P:(k + 1) * P],
                                             ring[:, 2 * which + k // 4, (k % 4) * DE:(k % 4 + 1) * DE], start=(k == 0), stop=(k == KD - 1))
                    last.then_inc(s_ov["gu"], 1)
                    pe.wait_ge(s_ov["h"], i + 1)
                    for c in range(4):
                        last = pe.transpose(psum[:, 4, c * P:(c + 1) * P], hh[:, c::4], ident)
                    last.then_inc(s_ov["ht"], 1)
                    pe.wait_ge(s_ov["htsb"], i + 1)
                    for dhalf in range(2):
                        for c in range(4):
                            last = pe.matmul(bank(5 + dhalf), flat(7)[:, c * P:(c + 1) * P],
                                             ring[:, 4 + c // 2, (c % 2) * D + dhalf * 512:(c % 2) * D + dhalf * 512 + 512],
                                             start=(c == 0), stop=(c == 3))
                    last.then_inc(s_ov["y"], 1)

        @block.scalar
        def _(act):
            def hi(u):
                act.wait_ge(s_raw[u % MIX_RING], 16 * (u // MIX_RING) + 16)
                if u >= WBUF:
                    act.wait_ge(s_used, u - WBUF + 1)
                act.activation(w_hi[:, u % WBUF, :], ring[:, u % MIX_RING, :], ACT.Copy).then_inc(s_hi, 1)

            hi(0)
            for k in range(KD):
                act.wait_ge(s_xt, k + 1)
                act.activation(act_hi[:, k, :], bank(k), ACT.Copy).then_inc(s_xthi, 1)
            act.wait_ge(s_lbready, 1)
            act.activation(lbe, lbe, ACT.Exp).then_inc(s_lnf, 1)
            for u in range(1, 4):
                hi(u)
            for half in range(2):
                act.wait_ge(s_strip, half + 1)
                n = 512 if half == 0 else P
                act.activation(strip_sb[:, 512 * half:512 * half + n], psum[0:HEADS, 7 - half, 0:n], ACT.Copy, scale=-1.0).then_inc(s_stripsb, 1)
            act.wait_ge(s_used, 2)
            act.activation(flat(8), banks(0, 4), ACT.Sigmoid).then_inc(s_evac, 1)
            hi(4)
            act.wait_ge(s_evac, 1)
            act.wait_ge(s_lbready, 2)
            for a in range(PAIRS):
                act.activation(logf[:, a, :], qe[:, a, :], ACT.Ln, scale=oml[:, a:a + 1], bias=lb[:, a:a + 1]).then_inc(s_lnf, 1)
            hi(5)
            act.wait_ge(s_used, 4)
            act.activation(flat(3), banks(4, 4), ACT.Silu).then_inc(s_evac, 1)
            hi(6)
            act.wait_ge(s_kk, PAIRS)
            act.wait_ge(s_scan, PAIRS)
            act.activation(flat(8), flat(5), ACT.Exp).then_inc(s_eb, 1)
            act.activation(flast, hb[:, :, CH - 1::CH], ACT.Exp).then_inc(s_eb, 1)
            act.wait_ge(s_d, 1)
            act.activation(flat(6), flat(6), ACT.Exp, scale=-1.0).then_inc(s_ed, 1)
            hi(7)
            act.wait_ge(s_used, 6)
            act.activation(flat(11), banks(0, 4), ACT.Copy).then_inc(s_evac, 1)
            hi(8)

            def level(l):
                m = LEVELS[l]
                act.wait_ge(s_d, l + 2)
                v = flat([7, 6][l % 2]).rearrange("p (n s) -> p n s", s=2 * m)
                act.activation(v[:, :, 0:m], v[:, :, 0:m], ACT.Exp, scale=-1.0).then_inc(s_ed, 1)
                act.activation(v[:, :, m:2 * m], v[:, :, m:2 * m], ACT.Exp).then_inc(s_ed, 1)

            level(0)
            hi(9)
            act.wait_ge(s_used, 8)
            act.activation(misc[:, 1024:3072], banks(4, 4), ACT.Sigmoid).then_inc(s_evac, 1)
            hi(10)
            act.wait_ge(s_scan, PAIRS)
            for i in range(T):
                act.wait_ge(s_ket, i + 1)
                act.activation(ke_tok[:, i, :], bank(2 + i % 2), ACT.Copy).then_inc(s_ketok, 1)
            for l in range(1, len(LEVELS)):
                level(l)
            act.wait_ge(s_copied, GROUPS)
            act.wait_ge(s_zero, 2)
            for h in range(HEADS):
                a, par = h // 2, h % 2
                if h >= 2:
                    act.wait_ge(s_abdfree, h - 1)
                for c in range(2):
                    rows = slice(64 * c, 64 * c + 64)
                    src = amat[rows, 2 * (a // 2) + par, (a % 2) * 256:(a % 2) * 256 + 256].rearrange("p (i t) -> p i t", i=T)
                    last = act.activation(abd[rows, h % 2, :, 64 * c:64 * c + 64], src, ACT.Copy)
                    if c == 0:
                        last.then_inc(s_act, 1)
                last.then_inc(s_abd, 1)
            for i in range(T):
                act.wait_ge(s_av, i + 1)
                if i >= 1:
                    act.wait_ge(s_ms, i)
                act.activation(sq[:, 0:512], bank(4 + i), ACT.Square).then_inc(s_sq, 1)
            act.wait_ge(s_ms, T + 1)
            act.activation(rs, ms, ACT.Sqrt).then_inc(s_sqrt, 1)
            hi(11)
            act.wait_ge(s_used, 10)
            act.activation(flat(5).rearrange("p (n q) -> p n q", q=P), turned(banks(0, 4)), ACT.Copy, scale=-SCALE).then_inc(s_evac, 1)
            hi(12)
            hi(13)
            act.wait_ge(s_used, 12)
            act.wait_ge(s_ms, T + 1)
            act.activation(flat(6), banks(4, 4), ACT.Copy).then_inc(s_evac, 1)
            hi(14)
            hi(15)
            act.wait_ge(s_used, 14)
            act.activation(flat(7), banks(0, 4), ACT.Copy).then_inc(s_evac, 1)
            hi(16)
            NU = HEADS * T

            def probs(n):
                h, i = n // T, n % T
                act.wait_ge(s_logit, n + 1)
                act.activation(p_buf(h, i), p_buf(h, i), ACT.Exp, scale=-1.0, bias=nmax[:, n:n + 1], accum_out=psums[:, n:n + 1]).then_inc(s_prob, 1)

            def pt_copy(n):
                h, i = n // T, n % T
                act.wait_ge(s_pt, n + 1)
                if h >= 2:
                    act.wait_ge(s_pv, n - 2 * T + 1)
                act.activation(pt_buf(h, i), psum[:, 6 + n % 2, 0:P * (i + 1)], ACT.Copy).then_inc(s_ptsb, 1)

            for n in range(NU + 1):
                if n < NU:
                    probs(n)
                if n >= 1:
                    pt_copy(n - 1)
            for n in range(KD):
                k = (4 + n) % KD
                act.wait_ge(s_mixt, n + 1)
                src = bank(4 + n % 4).rearrange("p (i q) -> p i q", q=P) if k >= 4 else turned(bank(4 + n % 4))
                act.activation(act_hi[:, k, :].rearrange("p (i q) -> p i q", q=P), src, ACT.Copy).then_inc(s_mixthi, 1)
            hi(17)

            def ehi(v0, j):
                slot = (v0 + 3) % RING
                before = 1 + v0 // RING + (MIX_UNITS // MIX_RING if slot < MIX_RING else 0)
                act.wait_ge(s_raw[slot], 16 * before + 16 * j)
                act.wait_ge(s_used, MIX_UNITS + v0 - WBUF + 1 + 12 * j)
                act.activation(w_hi[:, v0 % WBUF, :], ring[:, slot, :], ACT.Copy).then_inc(s_hi, 1)

            ehi(0, 0)
            ehi(1, 0)
            act.wait_ge(s_eps, 2)
            for i in range(T):
                act.wait_ge(s_var, i + 1)
                act.activation(rstd[:, i:i + 1], mv[:, i, 1:2], ACT.Sqrt, bias=eps_ln).then_inc(s_std, 1)
                act.wait_ge(s_ln, i + 1)
                act.activation(x_res[:, i, :], x_res[:, i, :], ACT.Identity, scale=rstd[:, i:i + 1], bias=nmr[:, i:i + 1]).then_inc(s_x1n, 1)
                act.wait_ge(s_x1t, i + 1)
                if i >= 2:
                    act.wait_ge(s_logits, i - 1)
                act.activation(misc[:, (i % 2) * D:(i % 2) * D + D], banks(2 * i, 2), ACT.Copy).then_inc(s_x1tsb, 1)
            ehi(2, 0)
            act.wait_ge(s_rneed, 1)
            act.activation(r_ge, r_ge, ACT.Exp).then_inc(s_rexp, 1)
            act.wait_ge(s_rneed, 2)
            act.activation(r_ee, r_ee, ACT.Exp).then_inc(s_rexp, 1)

            def xt_hi(e, b):
                act.wait_ge(s_et, e + 1)
                act.activation(e_hi[:, b, :], banks(0, 2), ACT.Copy).then_inc(s_ethi, 1)

            def silu(e, v0, j):
                act.wait_ge(s_used, MIX_UNITS + v0 + 12 * j)
                act.activation(gs, bank(2), ACT.Silu).then_inc(s_silu, 1)

            def ht_hi(s):
                act.wait_ge(s_ht, s)
                act.activation(h_hi, bank(4), ACT.Copy).then_inc(s_hthi, 1)

            def y_out(e, b, v0, j):
                act.wait_ge(s_used, MIX_UNITS + v0 + 12 * j)
                if not (isinstance(e, int) and e < 2):
                    act.wait_ge(s_yout[b], 8 * (e - b))
                act.activation(yb[:, b, :], banks(5, 2), ACT.Copy).then_inc(s_y, 1)

            def step(s0, j, following=True, ahead=True):
                s, b, v = s0 + 2 * j, s0 % 2, 4 + 6 * (s0 - 1)
                ehi(v + 3, j)
                ht_hi(s)
                ehi(v + 4, j)
                silu(s, v + 2, j)
                ehi(v + 5, j)
                y_out(s - 1, 1 - b, v + 4, j)
                if following:
                    xt_hi(s + 1, 1 - b)
                ehi(v + 6, j)
                ehi(v + 7, j)
                if ahead:
                    ehi(v + 8, j)

            xt_hi(0, 0)
            ehi(3, 0)
            ehi(4, 0)
            silu(0, 2, 0)
            xt_hi(1, 1)
            ehi(5, 0)
            ehi(6, 0)
            step(1, 0)
            with act.Fori(0, NE // 2 - 2) as j:
                step(2, j)
                step(3, j)
            step(NE - 2, 0)
            step(NE - 1, 0, following=False, ahead=False)
            ht_hi(NE)
            y_out(NE - 1, 1, 6 * NE, 0)

            act.wait_ge(s_flag, 2)
            over = act.value_load(over_i[0:1, 0:1], min_val=0, max_val=1)
            with act.If(over > 0):
                act.wait_ge(s_yout[0], 16 * (NE // 2))
                with act.Fori(0, ROUNDS * NE) as i:
                    act.wait_ge(s_ov["xt"], i + 1)
                    act.activation(flat(6)[:, 0:D], banks(0, 2), ACT.Copy).then_inc(s_ov["xtsb"], 1)
                    act.wait_ge(s_ov["gu"], i + 1)
                    act.activation(gs, bank(2), ACT.Silu).then_inc(s_ov["silu"], 1)
                    act.wait_ge(s_ov["ht"], i + 1)
                    act.activation(flat(7)[:, 0:512], bank(4), ACT.Copy).then_inc(s_ov["htsb"], 1)
                    act.wait_ge(s_ov["y"], i + 1)
                    act.activation(yb[:, 0, :], banks(5, 2), ACT.Copy).then_inc(s_ov["ysb"], 1)

            act.wait_ge(s_xo, 16)
            act.activation(f_x1[:, :, :], f_x1[:, :, :], ACT.Copy, scale=ALPHA).then_inc(s_ft, 1)
            for i in range(T):
                act.wait_ge(s_fv, i + 1)
                act.activation(rstd[:, i:i + 1], mv[:, i, 1:2], ACT.Sqrt, bias=eps_ln).then_inc(s_fs, 1)
                act.wait_ge(s_fl, i + 1)
                act.activation(f_x1[:, i, :], f_x1[:, i, :], ACT.Identity, scale=rstd[:, i:i + 1], bias=nmr[:, i:i + 1]).then_inc(s_fn, 1)

        @block.vector
        def _(dve):
            links = [0]

            def link(ins):
                links[0] += 1
                ins.then_inc(s_dve, 1)
                dve.wait_ge(s_dve, links[0])

            def lo(u):
                dve.wait_ge(s_hi, u + 1)
                if u >= WBUF:
                    dve.wait_ge(s_used, u - WBUF + 1)
                dve.tensor_tensor(w_lo[:, u % WBUF, :], ring[:, u % MIX_RING, :], w_hi[:, u % WBUF, :].bitcast(F32), ALU.subtract).then_inc(s_lo, 1)

            dve.memset(tab[N_BUCKETS:N_BUCKETS + 1, :], -BIG).then_inc(s_flag, 1)
            dve.memset(eps_ln, LN_EPS).then_inc(s_eps, 1)
            dve.memset(eps_rms, RMS_EPS).then_inc(s_eps, 1)
            dve.wait_ge(s_lb, 16)
            link(dve.tensor_tensor(lbm, lb2[:, 0, :], lb2[:, 1, :], ALU.max))
            dve.tensor_tensor(lbe[:, 0, :], lb2[:, 0, :], lbm, ALU.subtract)
            dve.tensor_tensor(lbe[:, 1, :], lb2[:, 1, :], lbm, ALU.subtract).then_inc(s_lbready, 1)
            lo(0)
            for k in range(KD):
                dve.wait_ge(s_xthi, k + 1)
                dve.tensor_tensor(act_lo[:, k, :], bank(k), act_hi[:, k, :].bitcast(F32), ALU.subtract).then_inc(s_xtlo, 1)
            dve.wait_ge(s_lnf, 1)
            link(dve.tensor_tensor(lbs, lbe[:, 0, :], lbe[:, 1, :], ALU.add))
            link(dve.reciprocal(lbs, lbs))
            link(dve.tensor_tensor(lb, lbe[:, 0, :], lbs, ALU.mult))
            link(dve.tensor_scalar(lb, lb, F_FLOOR, None, ALU.max))
            link(dve.tensor_scalar(oml, lb, -1.0, 1.0, ALU.mult, ALU.add))
            dve.tensor_scalar(noml, oml, -1.0, None, ALU.mult).then_inc(s_lbready, 1)
            lo(1)
            lo(2)
            lo(3)
            lo(4)
            dve.wait_ge(s_evac, 1)
            dve.wait_ge(s_lbready, 2)
            for a in range(PAIRS):
                dve.tensor_scalar(hk[:, a, :], qe[:, a, :], noml[:, a:a + 1], oml[:, a:a + 1], ALU.mult, ALU.add).then_inc(s_kk, 1)
            for a in range(PAIRS):
                dve.wait_ge(s_lnf, a + 2)
                dve.tensor_tensor_scan(hb[:, a, :], cst[:, C_SCAN:C_SCAN + SEQ], logf[:, a, :], 0.0, ALU.mult, ALU.add).then_inc(s_scan, 1)
            lo(5)
            lo(6)
            dve.wait_ge(s_evac, 2)
            dve.wait_ge(s_eb, 1)
            dve.tensor_tensor(flat(8), flat(8), flat(3), ALU.mult).then_inc(s_qe, 1)
            dve.wait_ge(s_ed, 1)
            dve.wait_ge(s_kk, PAIRS)
            dve.tensor_tensor(flat(6), flat(6), flat(4), ALU.mult).then_inc(s_ke, 1)
            lo(7)
            dve.wait_ge(s_stripd, 16)
            dve.memset(misc[:, 0:1024], 0.0).then_inc(s_zero, 1)
            dve.memset(flat(10), 0.0).then_inc(s_memz, 1)
            dve.memset(misc[:, 3072:4096], 0.0).then_inc(s_zero, 1)
            lo(8)

            def level(l):
                m = LEVELS[l]
                dve.wait_ge(s_ed, 2 * l + 3)
                view = lambda f: f.rearrange("p (n s) -> p n s", s=2 * m)
                v, k, q = view(flat([7, 6][l % 2])), view(flat(4)), view(flat(3))
                dve.tensor_tensor(v[:, :, 0:m], v[:, :, 0:m], k[:, :, 0:m], ALU.mult).then_inc(s_half, 1)
                dve.tensor_tensor(v[:, :, m:2 * m], v[:, :, m:2 * m], q[:, :, m:2 * m], ALU.mult).then_inc(s_w, 1)

            def keep(g):
                lev = g // 4
                dve.wait_ge(s_prod, g + 1)
                if g == 0:
                    dve.wait_ge(s_memz, 1)
                if lev > 0:
                    dve.wait_ge(s_copied, g - 3)
                mask = cst[:, C_MASK + 64 * lev:C_MASK + 64 * lev + 64].bitcast(U32).rearrange("p (a t) -> p a t", a=1).broadcast_to((P, 8, 64))
                dve.copy_predicated(amat[:, g % 4, :].rearrange("p (n t) -> p n t", t=64), mask,
                                    bank(g % 2).rearrange("p (n t) -> p n t", t=64)).then_inc(s_copied, 1)

            level(0)
            lo(9)
            lo(10)
            dve.wait_ge(s_eb, 2)
            dve.wait_ge(s_zero, 2)
            for c in range(NCH):
                keep(c)
                if c < NCH - 1:
                    dve.wait_ge(s_kv, c + 1)
                    if c >= 1:
                        dve.wait_ge(s_inter, c)
                    for hh2 in range(2):
                        rows = slice(64 * hh2, 64 * hh2 + 64)
                        now, nxt = state[rows, c % 2, :, rows], state[rows, (c + 1) % 2, :, rows]
                        dec = flast[rows, :, c:c + 1].broadcast_to((64, PAIRS, 64))
                        dve.tensor_tensor(nxt, now, dec, ALU.mult).then_inc(s_st1, 1)
                    for hh2 in range(2):
                        rows = slice(64 * hh2, 64 * hh2 + 64)
                        nxt = state[rows, (c + 1) % 2, :, rows]
                        kv = bank(2 + c % 2).rearrange("p (a v) -> p a v", a=PAIRS)[rows, :, rows]
                        dve.wait_ge(s_st1, 2 * c + 1 + hh2)
                        ins = dve.tensor_tensor(nxt, nxt, kv, ALU.add)
                        if hh2 == 0:
                            ins.then_inc(s_st2, 1)
                    ins.then_inc(s_state, 1)
                    dve.wait_ge(s_state, c + 1)
                    dve.wait_ge(s_st2, c + 1)
            level(1)
            for g in range(8, GROUPS):
                if g % 4 == 0 and g // 4 < len(LEVELS):
                    level(g // 4)
                keep(g)
            for i in range(T):
                dve.wait_ge(s_sq, i + 1)
                dve.tensor_reduce(ms[:, 8 * i:8 * i + 8], sq[:, 0:512].rearrange("p (h v) -> p h v", v=DH), AX.X, ALU.add).then_inc(s_ms, 1)
            dve.wait_ge(s_ms, T)
            dve.tensor_scalar(ms, ms, 1.0 / DH, RMS_EPS, ALU.mult, ALU.add).then_inc(s_ms, 1)
            dve.wait_ge(s_sqrt, 1)
            link(dve.reciprocal(rs, rs))
            for i in range(T):
                scale = rs[:, 8 * i:8 * i + 8].rearrange("p (h a) -> p h a", a=1).broadcast_to((P, HEADS, DH))
                dve.tensor_tensor(mix_r[:, i, :].rearrange("p (h v) -> p h v", v=DH), bank(4 + i).rearrange("p (h v) -> p h v", v=DH),
                                  scale, ALU.mult).then_inc(s_r, 1)
            dve.wait_ge(s_gate, T)
            for i in range(T):
                dve.wait_ge(s_r, i + 1)
                dve.tensor_tensor(mix_r[:, i, :], mix_r[:, i, :], gate[:, i, :], ALU.mult).then_inc(s_mixr, 1)
            for u in range(11, 17):
                lo(u)
            NU = HEADS * T
            dve.wait_ge(s_strips, 16 * HEADS)
            dve.wait_ge(s_evac, 7)
            for n in range(NU):
                h, i = n // T, n % T
                dve.wait_ge(s_score, n + 1)
                if h >= 2:
                    dve.wait_ge(s_pt, n - 2 * T + 1)
                w = P * (i + 1)
                dve.tensor_tensor_reduce(p_buf(h, i), psum[:, 4 + n % 2, 0:w], strips[:, h, SEQ - w:SEQ], 1.0, 3.0e38,
                                         ALU.add, ALU.min, nmax[:, n:n + 1]).then_inc(s_logit, 1)
            dve.wait_ge(s_prob, NU)
            link(dve.reciprocal(prec, psums))
            for i in range(T):
                dve.wait_ge(s_pv, NU - T + i + 1)
                scale = prec.rearrange("p (h i a) -> p i h a", i=T, a=1)[:, i, :, :].broadcast_to((P, HEADS, DH))
                dve.tensor_tensor(mix_a[:, i, :].rearrange("p (h v) -> p h v", v=DH), bank(i).rearrange("p (h v) -> p h v", v=DH),
                                  scale, ALU.mult).then_inc(s_mixa, 1)
            for n in range(KD):
                k = (4 + n) % KD
                dve.wait_ge(s_mixthi, n + 1)
                src = bank(4 + n % 4).rearrange("p (i q) -> p i q", q=P) if k >= 4 else turned(bank(4 + n % 4))
                dve.tensor_tensor(act_lo[:, k, :].rearrange("p (i q) -> p i q", q=P), src,
                                  act_hi[:, k, :].bitcast(F32).rearrange("p (i q) -> p i q", q=P), ALU.subtract).then_inc(s_mixtlo, 1)
            lo(17)

            def elo(v0, j):
                slot = (v0 + 3) % RING
                dve.wait_ge(s_hi, MIX_UNITS + v0 + 1 + 12 * j)
                dve.wait_ge(s_used, MIX_UNITS + v0 - WBUF + 1 + 12 * j)
                dve.tensor_tensor(w_lo[:, v0 % WBUF, :], ring[:, slot, :], w_hi[:, v0 % WBUF, :].bitcast(F32), ALU.subtract).then_inc(s_lo, 1)

            elo(0, 0)
            elo(1, 0)
            dve.wait_ge(s_xres, 16)
            dve.wait_ge(s_lnw, 32)

            def shift_scale(i):
                link(dve.reciprocal(rstd[:, i:i + 1], rstd[:, i:i + 1]))
                return dve.scalar_tensor_tensor(out=nmr[:, i:i + 1], in0=mv[:, i, 0:1], scalar=-1.0, in1=rstd[:, i:i + 1], op0=ALU.mult, op1=ALU.mult)

            def stats(x, i):
                for half in range(2):
                    dve.bn_stats(bst[:, i, half, :], x[:, 512 * half:512 * half + 512]).then_inc(s_bn, 1)

            def scaled(i):
                dve.wait_ge(s_x1n, i + 1)
                dve.tensor_tensor(x_res[:, i, :], x_res[:, i, :], lng, ALU.mult).then_inc(s_lg, 1)
                dve.wait_ge(s_lg, i + 1)
                dve.tensor_tensor(x_res[:, i, :], x_res[:, i, :], lnb, ALU.add).then_inc(s_x1, 1)

            def routed(i):
                dve.wait_ge(s_logits, i + 1)
                dve.tensor_tensor(r_l[:, i, :], psum[:, 2 * i, 0:NL], rbias, ALU.add).then_inc(s_lin, 1)

            dve.wait_ge(s_small, 48)
            for i in range(T):
                if i < T - 1:
                    dve.wait_ge(s_wo, i + 1)
                else:
                    dve.wait_ge(s_used, MIX_UNITS)
                for half in range(2):
                    xs = x_res[:, i, 512 * half:512 * half + 512]
                    dve.scalar_tensor_tensor(out=xs, in0=xs, scalar=ALPHA, in1=bank(2 * i + half), op0=ALU.mult, op1=ALU.add).then_inc(s_res, 1)
                dve.wait_ge(s_res, 2 * i + 2)
                stats(x_res[:, i, :], i)
                dve.wait_ge(s_bn, 2 * i + 2)
                dve.bn_aggr(mv[:, i, :], bst[:, i, :, :].rearrange("p b n -> p (b n)")).then_inc(s_var, 1)
                dve.wait_ge(s_std, i + 1)
                dve.wait_ge(s_var, i + 1)
                shift_scale(i).then_inc(s_ln, 1)
                scaled(i)
                if i >= 1:
                    routed(i - 1)
            routed(T - 1)
            elo(2, 0)
            if stage == "x1":
                return

            def bc(ap, n):
                return ap.broadcast_to((P, T, n))

            dve.wait_ge(s_lin, T)
            gl = r_l[:, :, 0:NG]
            link(dve.tensor_reduce(r_m, gl, AX.X, ALU.max))
            dve.tensor_tensor(r_g, gl, bc(r_m, NG), ALU.subtract).then_inc(s_rneed, 1)
            dve.wait_ge(s_rexp, 1)
            w4 = cst[:, C_W4:C_W4 + 4].rearrange("p (a n) -> p a n", a=1)

            def first_max(e, hot, top):
                link(dve.tensor_reduce(top, e, AX.X, ALU.max))
                link(dve.tensor_tensor(hot, e, bc(top, 4), ALU.is_equal))
                link(dve.tensor_tensor(hot, hot, bc(w4, 4), ALU.mult))
                link(dve.tensor_reduce(r_m, hot, AX.X, ALU.max))
                link(dve.tensor_tensor(hot, hot, bc(r_m, 4), ALU.is_equal))

            link(dve.tensor_reduce(r_gsum, r_g, AX.X, ALU.add))
            link(dve.reciprocal(r_gw, r_gsum))
            first_max(r_g, r_gh, r_top)
            for g in range(NG):
                dst = r_e if g == 0 else r_tmp
                link(dve.tensor_tensor(dst, r_l[:, :, NG + EPG * g:NG + EPG * g + EPG], bc(r_gh[:, :, g:g + 1], EPG), ALU.mult))
                if g:
                    link(dve.tensor_tensor(r_e, r_e, r_tmp, ALU.add))
            link(dve.tensor_reduce(r_m, r_e, AX.X, ALU.max))
            dve.tensor_tensor(r_e, r_e, bc(r_m, EPG), ALU.subtract).then_inc(s_rneed, 1)
            dve.wait_ge(s_rexp, 2)
            first_max(r_e, r_h[:, 0], r_top)
            link(dve.scalar_tensor_tensor(out=r_tmp, in0=r_h[:, 0], scalar=-2.0, in1=r_e, op0=ALU.mult, op1=ALU.add))
            first_max(r_tmp, r_h[:, 1], r_top2)
            link(dve.tensor_tensor(r_gsum, r_top, r_top2, ALU.add))
            link(dve.reciprocal(r_gsum, r_gsum))
            link(dve.tensor_tensor(r_gw, r_gw, r_gsum, ALU.mult))
            link(dve.tensor_tensor(wgt[:, :, 0:1], r_gw, r_top, ALU.mult))
            link(dve.tensor_tensor(wgt[:, :, 1:2], r_gw, r_top2, ALU.mult))
            for k in range(2):
                for g in range(NG):
                    link(dve.tensor_tensor(r_sel[:, k, :, EPG * g:EPG * g + EPG], r_h[:, k], bc(r_gh[:, :, g:g + 1], EPG), ALU.mult))
            dve.tensor_tensor(r_msk, r_sel[:, 0], r_sel[:, 1], ALU.add).then_inc(s_mask, 1)
            dve.wait_ge(s_pos, 1)
            pos = psum[:, 7, 0:T * NE].rearrange("p (i e) -> p i e", i=T)
            e16 = cst[:, C_E16:C_E16 + NE].rearrange("p (a e) -> p a e", a=1)
            link(dve.tensor_scalar(r_pos, pos, float(NE), None, ALU.mult))
            link(dve.tensor_tensor(r_pos, r_pos, bc(e16, NE), ALU.add))
            for k in range(2):
                link(dve.tensor_tensor(r_t16, r_pos, r_sel[:, k], ALU.mult))
                link(dve.tensor_reduce(r_adr[:, :, k:k + 1], r_t16, AX.X, ALU.add))
            dve.tensor_copy(addr_i[:, :, :], r_adr).then_inc(s_addr, 1)
            link(dve.tensor_reduce(r_cnt, psum[:, 7, T * NE:(T + 1) * NE], AX.X, ALU.max))
            link(dve.tensor_scalar(r_cnt, r_cnt, float(CAP), None, ALU.is_gt))
            dve.tensor_copy(over_i[:, :], r_cnt).then_inc(s_flag, 1)

            def xt_lo(e, b):
                dve.wait_ge(s_ethi, e + 1)
                dve.tensor_tensor(e_lo[:, b, :], banks(0, 2), e_hi[:, b, :].bitcast(F32), ALU.subtract).then_inc(s_etlo, 1)

            def hidden(e, v0, j):
                dve.wait_ge(s_used, MIX_UNITS + v0 + 12 * j)
                dve.wait_ge(s_silu, e + 1)
                dve.tensor_tensor(hh, bank(3), gs, ALU.mult).then_inc(s_h, 1)

            def step(s0, j, following=True, ahead=True):
                s, b, v = s0 + 2 * j, s0 % 2, 4 + 6 * (s0 - 1)
                elo(v + 3, j)
                dve.wait_ge(s_hthi, s)
                dve.tensor_tensor(h_lo, bank(4), h_hi.bitcast(F32), ALU.subtract).then_inc(s_htlo, 1)
                elo(v + 4, j)
                elo(v + 5, j)
                if following:
                    xt_lo(s + 1, 1 - b)
                elo(v + 6, j)
                elo(v + 7, j)
                hidden(s, v + 6, j)
                if ahead:
                    elo(v + 8, j)

            xt_lo(0, 0)
            elo(3, 0)
            elo(4, 0)
            xt_lo(1, 1)
            elo(5, 0)
            hidden(0, 4, 0)
            elo(6, 0)
            step(1, 0)
            with dve.Fori(0, NE // 2 - 2) as j:
                step(2, j)
                step(3, j)
            step(NE - 2, 0)
            step(NE - 1, 0, following=False, ahead=False)
            dve.wait_ge(s_hthi, NE)
            dve.tensor_tensor(h_lo, bank(4), h_hi.bitcast(F32), ALU.subtract).then_inc(s_htlo, 1)

            dve.wait_ge(s_flag, 2)
            over = dve.value_load(over_i[0:1, 0:1], min_val=0, max_val=1)
            with dve.If(over > 0):
                with dve.Fori(0, ROUNDS * NE) as i:
                    dve.wait_ge(s_ov["silu"], i + 1)
                    dve.tensor_tensor(hh, bank(3), gs, ALU.mult).then_inc(s_ov["h"], 1)

            dve.wait_ge(s_ft, 1)
            dve.wait_ge(s_fw, 32)
            for i in range(T):
                dve.wait_ge(s_pairs[i], 16)
                y = f_x1[:, i, :]
                for k in range(2):
                    dve.scalar_tensor_tensor(out=y, in0=f_pair(i)[:, k * D:(k + 1) * D], scalar=wgt[:, i, k:k + 1], in1=y,
                                             op0=ALU.mult, op1=ALU.add).then_inc(s_facc, 1)
                    dve.wait_ge(s_facc, 2 * i + k + 1)
                stats(y, i)
                dve.wait_ge(s_bn, 2 * (T + i) + 2)
                dve.bn_aggr(mv[:, i, :], bst[:, i, :, :].rearrange("p b n -> p (b n)")).then_inc(s_fv, 1)
                dve.wait_ge(s_fs, i + 1)
                dve.wait_ge(s_fv, i + 1)
                shift_scale(i).then_inc(s_fl, 1)
                dve.wait_ge(s_fn, i + 1)
                dve.tensor_tensor(y, y, f_g, ALU.mult).then_inc(s_fm, 1)


SHAPES = {
    "x": (SEQ, D), "w_in": (D, 7 * WIDTH), "t5_bias": (N_BUCKETS, HEADS), "hgrn_lb_logits": (2, WIDTH), "hgrn_norm_w": (1, WIDTH),
    "w_o": (D, D), "ln1_g": (1, D), "ln1_b": (1, D), "w_group": (D, NG), "b_group": (1, NG), "w_expert": (NG, D, EPG),
    "b_expert": (1, NE), "w_gate": (NE, D, DE), "w_up": (NE, D, DE), "w_down": (NE, DE, D), "ln2_g": (1, D), "ln2_b": (1, D),
}
STAGE = ""


def kernel(**inputs):
    import concourse.bacc as bacc
    from concourse.bass_utils import run_bass_kernel_spmd as run

    nc = bacc.Bacc("TRN2", target_bir_lowering=False, num_devices=1)
    arrays, t = {}, {}
    main, hot = shape_constants()
    laid = {n: np.ascontiguousarray(inputs[n]).reshape(s) for n, s in SHAPES.items()}
    laid["c_main"], laid["c_hot"] = main, hot
    for n, a in laid.items():
        arrays["in_" + n] = a
        t[n] = nc.dram_tensor("in_" + n, a.shape, mybir.dt.from_np(a.dtype), kind="ExternalInput").ap()
    out = nc.dram_tensor("out", (SEQ, D), F32, kind="ExternalOutput").ap()
    build(nc, t, out, STAGE)
    return run(nc, [arrays], core_ids=[0]).results[0]["out"].reshape(1, SEQ, D)
```

```python
import math
from contextlib import ExitStack

import numpy as np

import concourse.bass as bass
from concourse import mybir

F32 = mybir.dt.float32
F32R = mybir.dt.float32r
I32 = mybir.dt.int32
U32 = mybir.dt.uint32
ALU = mybir.AluOpType
ACT = mybir.ActivationFunctionType
AX = mybir.AxisListType

P = 128
SEQ, D, WIDTH, HEADS, DH = 512, 1024, 512, 8, 64
T = SEQ // P
KD = D // P
PAIRS = HEADS // 2
CH = 64
NCH = SEQ // CH
N_BUCKETS, MAX_DISTANCE = 32, 128
NG, EPG, NE, DE = 4, 4, 16, 512
NL = NG + NE
LN_EPS, RMS_EPS = 1e-5, 1e-6
ALPHA = 2.0 ** 0.25
SCALE = DH ** -0.5
BIG = 1.0e30
STRIP = SEQ + P
F_FLOOR = 2.0 ** -63
CAP = 128
ROUNDS = SEQ // CAP - 1
OV_SLOTS = [0, 1, 2, 9, 10, 11]
PAD_PAIR = 4 * SEQ

UNIT = 2048
RING = 12
WBUF = 3
MIX_RING = 3
BLOCKS = [4, 3, 5, 6, 0, 2, 1]
WIN_UNITS = 2 * len(BLOCKS)
WO_UNITS = 4
MIX_UNITS = WIN_UNITS + WO_UNITS
LEVELS = [32, 16, 8, 4, 2, 1]
LEVEL_SLOTS = [7, 6, 9, 8, 7, 6]
GROUPS = 4 * (1 + len(LEVELS))

C_ID, C_TRI, C_ONE = 0, P, 2 * P
C_MASK = 3 * P
C_SCAN = C_MASK + 64 * (1 + len(LEVELS))
C_W4 = C_SCAN + SEQ
C_E16 = C_W4 + 4
C_PAIR = C_E16 + NE
C_PAD = C_PAIR + 4 * T
NC = C_PAD + 2 * NE


def shape_constants():
    c = np.zeros((P, NC), np.float32)
    c[:, C_ID:C_ID + P] = np.eye(P)
    c[:, C_TRI:C_TRI + P] = np.triu(np.ones((P, P)), 1)
    c[:, C_ONE:C_ONE + P] = 1
    s, t = np.arange(P)[:, None] % CH, np.arange(CH)[None, :]
    c[:, C_MASK:C_MASK + 64] = s == t
    for l, m in enumerate(LEVELS):
        c[:, C_MASK + 64 * (l + 1):C_MASK + 64 * (l + 2)] = (s // (2 * m) == t // (2 * m)) & (s % (2 * m) < m) & (t % (2 * m) >= m)
    c[:, C_SCAN:C_SCAN + SEQ] = (np.arange(SEQ) % CH != 0)[None]
    c[:, C_W4:C_W4 + 4] = [4, 3, 2, 1]
    c[:, C_E16:C_E16 + NE] = np.arange(NE)
    for i in range(T):
        tok = i * P + np.arange(P)
        for k in range(2):
            c[:, C_PAIR + 4 * i + 2 * k] = tok
            c[:, C_PAIR + 4 * i + 2 * k + 1] = 2 * tok + k
    c[:, C_PAD + 1::2] = PAD_PAIR
    n = SEQ - 1 - np.arange(STRIP)
    half = N_BUCKETS // 2
    nf = np.maximum(n, 1).astype(np.float32)
    large = half + (np.log(nf / half) / math.log(MAX_DISTANCE / half) * (N_BUCKETS - half)).astype(np.int32)
    bucket = np.where(n < half, np.maximum(n, 0), np.minimum(large, N_BUCKETS - 1))
    hot = np.zeros((N_BUCKETS + 1, STRIP), np.float32)
    hot[bucket, np.arange(STRIP)] = 1
    hot[N_BUCKETS] = n < 0
    return c, hot


def build(nc, t, out):
    with ExitStack() as ctx:
        def sb(name, shape, dt=F32):
            return ctx.enter_context(nc.sbuf_tensor(name, shape, dt))

        def sem(name):
            return ctx.enter_context(nc.semaphore(name))

        def sems(name, n):
            return [sem(f"{name}{i}") for i in range(n)]

        x1_dram = nc.dram_tensor("x1_dram", (SEQ, D), F32).ap()
        pair_dram = nc.dram_tensor("pair_dram", (2 * SEQ, D), F32).ap()
        slot_dram = nc.dram_tensor("slot_dram", (SEQ * NE, 2), I32).ap()
        strip_dram = nc.dram_tensor("strip_dram", (HEADS, STRIP), F32).ap()

        ring = sb("ring", [P, RING, UNIT])
        w_hi = sb("w_hi", [P, WBUF, UNIT], F32R)
        w_lo = sb("w_lo", [P, WBUF, UNIT], F32R)
        act_hi = sb("act_hi", [P, KD, SEQ], F32R)
        act_lo = sb("act_lo", [P, KD, SEQ], F32R)
        misc = sb("misc", [P, 5120])
        cst = sb("cst", [P, NC])
        nw = sb("nw", [P, WIDTH])
        small = sb("small", [P, 512])
        slots = sb("slots", [P, NE, 2], I32)
        ov_rec = sb("ov_rec", [P, 2], I32)
        rec_i = sb("rec_i", [P, T, 2, 2], I32)
        addr_i = sb("addr_i", [P, T, 2], I32)
        over_i = sb("over_i", [P, 1], I32)
        pad_i = sb("pad_i", [P, NE, 2], I32)
        wgt = sb("wgt", [P, T, 2])

        ident = cst[:, C_ID:C_ID + P]
        tri = cst[:, C_TRI:C_TRI + P]
        ones = cst[:, C_ONE:C_ONE + P]

        def flat(slot):
            return ring[:, slot, :]

        x_tok = ring[:, 10:12, :].rearrange("p a (b d) -> p (a b) d", d=D)
        hq = flat(3).rearrange("p (a s) -> p a s", a=PAIRS)
        hk = flat(4).rearrange("p (a s) -> p a s", a=PAIRS)
        hb = flat(5).rearrange("p (a s) -> p a s", a=PAIRS)
        wlev = [flat(n).rearrange("p (a s) -> p a s", a=PAIRS) for n in LEVEL_SLOTS]
        qe = flat(8).rearrange("p (a s) -> p a s", a=PAIRS)
        logf = flat(9).rearrange("p (a s) -> p a s", a=PAIRS)
        ke_tok = flat(9).rearrange("p (i c) -> p i c", i=T)
        amat = flat(10).rearrange("p (g n) -> p g n", g=4)
        hv = flat(11).rearrange("p (i c) -> p i c", i=T)
        mix_r = flat(3).rearrange("p (i c) -> p i c", i=T)
        sq = flat(6)
        state = misc[:, 0:1024].rearrange("p (b a v) -> p b a v", b=2, a=PAIRS)
        gate = misc[:, 1024:3072].rearrange("p (i c) -> p i c", i=T)
        aq = flat(5).rearrange("p (a s) -> p a s", a=PAIRS)
        aq_hi, aq_lo = act_hi[:, 4:8, :], act_lo[:, 4:8, :]
        ak_hi, ak_lo = act_hi[:, 0:4, :], act_lo[:, 0:4, :]
        av = flat(7).rearrange("p (i c) -> p i c", i=T)
        strips = ring[:, 8:10, :].rearrange("p a (h n) -> p (a h) n", n=SEQ)
        mix_a = misc[:, 1024:3072].rearrange("p (i c) -> p i c", i=T)
        qz = misc[:, 3072:5120].rearrange("p (a c h t) -> p a c h t", a=PAIRS, c=NCH, h=2)
        strip_sb = misc[0:HEADS, 3072:3072 + STRIP]
        x_res = ring[:, 9:11, :].rearrange("p a (b d) -> p (a b) d", d=D)
        lng = flat(11)[:, 0:D]
        lnb = flat(11)[:, D:2 * D]
        x1t = misc[:, 0:2048].rearrange("p (b k t) -> p b k t", b=2, k=KD)
        wr = misc[:, 2048:2048 + KD * NL].rearrange("p (k n) -> p k n", k=KD)
        rt = misc[:, 2304:5120]
        tab = misc[0:N_BUCKETS + 1, 4096:4104]
        hot = misc[0:N_BUCKETS + 1, 4104:4104 + STRIP]

        e_hi = act_hi[:, 0:4, :].rearrange("p (b k) t -> p b (k t)", b=2)
        e_lo = act_lo[:, 0:4, :].rearrange("p (b k) t -> p b (k t)", b=2)
        h_hi, h_lo = act_hi[:, 4, :], act_lo[:, 4, :]
        f_x1 = ring[:, 3:5, :].rearrange("p a (b d) -> p (a b) d", d=D)
        f_g, f_b = flat(5)[:, 0:D], flat(5)[:, D:2 * D]
        xg = misc[:, 0:2048].rearrange("p (b d) -> p b d", b=2)
        gs = misc[:, 2048:2560]
        hh = misc[:, 2560:3072]
        yb = misc[:, 3072:5120].rearrange("p (b d) -> p b d", b=2)

        NU = HEADS * T

        def unit(n):
            return 2 * (n // (2 * T)) + n % 2, (n // 2) % T

        def o_off(i):
            return P * (i * (i + 1) // 2)

        def p_buf(h, i):
            return flat(10 + h % 2)[:, o_off(i):o_off(i) + P * (i + 1)]

        def pt_buf(h, i):
            if h % 2 == 0:
                return flat(4)[:, o_off(i):o_off(i) + P * (i + 1)]
            if i < 3:
                return flat(10)[:, 1280 + o_off(i):1280 + o_off(i) + P * (i + 1)]
            return flat(4)[:, 1280:1280 + P * (i + 1)]

        def f_pair(i):
            return flat(6 + i)

        lb2 = small[:, 0:8].rearrange("p (r a) -> p r a", r=2)
        lbm = small[:, 8:12]
        lbe = small[:, 12:20].rearrange("p (r a) -> p r a", r=2)
        lbs = small[:, 20:24]
        lb = small[:, 24:28]
        oml = small[:, 28:32]
        noml = small[:, 32:36]
        flast = small[:, 40:72].rearrange("p (a c) -> p a c", a=PAIRS)
        ms = small[:, 72:104]
        rs = small[:, 104:136]
        nmax = small[:, 136:168]
        psums = small[:, 168:200]
        prec = small[:, 200:232]
        bst = small[:, 232:280].rearrange("p (i b n) -> p i b n", i=T, b=2)
        mv = small[:, 280:288].rearrange("p (i n) -> p i n", i=T)
        rstd = small[:, 288:292]
        nmr = small[:, 292:296]
        eps_ln = small[:, 296:297]
        eps_rms = small[:, 297:298]
        rbias = small[:, 300:320]

        r_at = [0]

        def rcol(*shape):
            n = int(np.prod(shape))
            v = rt[:, T * NE + r_at[0]:T * NE + r_at[0] + n]
            r_at[0] += n
            names = "abcd"[:len(shape)]
            return v.rearrange("p (%s) -> p %s" % (" ".join(names), " ".join(names)), **dict(zip(names, shape)))

        r_msk = rt[:, 0:T * NE].rearrange("p (i e) -> p i e", i=T)
        r_l, r_m, r_g, r_gh, r_e, r_tmp = rcol(T, NL), rcol(T, 1), rcol(T, NG), rcol(T, NG), rcol(T, EPG), rcol(T, EPG)
        r_gsum, r_gw, r_top, r_top2 = rcol(T, 1), rcol(T, 1), rcol(T, 1), rcol(T, 1)
        r_h, r_sel, r_pos, r_t16, r_adr, r_cnt = rcol(2, T, EPG), rcol(2, T, NE), rcol(T, NE), rcol(T, NE), rcol(T, 2), rcol(1)
        r_ge, r_ee = r_g, r_e

        psum = ctx.enter_context(nc.psum_tensor("psum", [P, 8, 512], F32))

        s_ident, s_const, s_x, s_lb, s_small = sem("s_ident"), sem("s_const"), sem("s_x"), sem("s_lb"), sem("s_small")
        s_raw = sems("s_raw", RING)
        s_hi, s_lo, s_used = sem("s_hi"), sem("s_lo"), sem("s_used")
        s_xt, s_xthi, s_xtlo = sem("s_xt"), sem("s_xthi"), sem("s_xtlo")
        s_evac = sem("s_evac")
        s_dve, s_pool = sem("s_dve"), sem("s_pool")
        s_lbready, s_lnf, s_kk, s_scan = sem("s_lbready"), sem("s_lnf"), sem("s_kk"), sem("s_scan")
        s_eb, s_d, s_ed, s_qe, s_ke = sem("s_eb"), sem("s_d"), sem("s_ed"), sem("s_qe"), sem("s_ke")
        s_w, s_qz, s_zero = sem("s_w"), sem("s_qz"), sem("s_zero")
        s_ket, s_ketok, s_kv, s_state = sem("s_ket"), sem("s_ketok"), sem("s_kv"), sem("s_state")
        s_prod, s_copied, s_qkhi, s_qklo, s_av = sem("s_prod"), sem("s_copied"), sem("s_qkhi"), sem("s_qklo"), sem("s_av")
        s_sq, s_ms, s_sqrt, s_r, s_gate = sem("s_sq"), sem("s_ms"), sem("s_sqrt"), sem("s_r"), sem("s_gate")
        s_tab, s_strip, s_stripsb, s_stripd, s_strips = sem("s_tab"), sem("s_strip"), sem("s_stripsb"), sem("s_stripd"), sem("s_strips")
        s_score, s_logit, s_prob, s_pt, s_ptsb, s_pv, s_mixa = sem("s_score"), sem("s_logit"), sem("s_prob"), sem("s_pt"), sem("s_ptsb"), sem("s_pv"), sem("s_mixa")
        s_mixt, s_mixthi, s_mixtlo = sem("s_mixt"), sem("s_mixthi"), sem("s_mixtlo")
        s_wo, s_xres, s_ln, s_lnw, s_var, s_std, s_x1 = sem("s_wo"), sem("s_xres"), sem("s_ln"), sem("s_lnw"), sem("s_var"), sem("s_std"), sem("s_x1")
        s_x1out, s_x1t, s_x1tsb, s_logits, s_wr = sem("s_x1out"), sem("s_x1t"), sem("s_x1tsb"), sem("s_logits"), sem("s_wr")
        s_inter, s_mixr, s_flag = sem("s_inter"), sem("s_mixr"), sem("s_flag")
        s_cent, s_x1last, s_finlast, s_sel, s_lin, s_rexp, s_mask, s_pos, s_addr = sem("s_cent"), sem("s_x1last"), sem("s_finlast"), sem("s_sel"), sem("s_lin"), sem("s_rexp"), sem("s_mask"), sem("s_pos"), sem("s_addr")
        s_pads, s_slotw, s_slots = sem("s_pads"), sem("s_slotw"), sem("s_slots")
        s_out, s_eps, s_x1n, s_rneed, s_memz, s_half = sem("s_out"), sem("s_eps"), sem("s_x1n"), sem("s_rneed"), sem("s_memz"), sem("s_half")
        s_gidx, s_sidx, s_st1, s_st2, s_bn, s_lg, s_res = sem("s_gidx"), sem("s_sidx"), sem("s_st1"), sem("s_st2"), sem("s_bn"), sem("s_lg"), sem("s_res")
        s_fw, s_facc, s_fl, s_fn, s_fm = sem("s_fw"), sem("s_facc"), sem("s_fl"), sem("s_fn"), sem("s_fm")
        s_xg = sems("s_xg", 2)
        s_et, s_ethi, s_etlo = sem("s_et"), sem("s_ethi"), sem("s_etlo")
        s_silu, s_h, s_ht, s_hthi, s_htlo = sem("s_silu"), sem("s_h"), sem("s_ht"), sem("s_hthi"), sem("s_htlo")
        s_y = sem("s_y")
        s_yout = sems("s_yout", 2)
        s_ov = {n: sem(f"s_ov_{n}") for n in ("turn", "free", "idx", "w", "xg", "xt", "xtsb", "gu", "silu", "h", "ht", "htsb", "y", "ysb", "yout")}
        s_pairs = sems("s_pairs", 2 * T)
        s_xo, s_fin, s_fv, s_fs, s_ft = sem("s_xo"), sem("s_fin"), sem("s_fv"), sem("s_fs"), sem("s_ft")

        w_in = t["w_in"].rearrange("(p k) (b n) -> p k b n", p=P, n=WIDTH)
        w_o = t["w_o"].rearrange("(k p) d -> p k d", p=P)
        wg = t["w_gate"].rearrange("e (p k) f -> e p (k f)", p=P)
        wu = t["w_up"].rearrange("e (p k) f -> e p (k f)", p=P)
        wd = t["w_down"].rearrange("e (p c) d -> e p (c d)", p=P)

        def bank(b, n=512):
            return psum[:, b, 0:n]

        def banks(b, n):
            return psum[:, b:b + n, :].rearrange("p b n -> p (b n)")

        def turned(ap):
            return ap.rearrange("p (n q) -> p n q", q=P)[:, :, ::-1]

        block = ctx.enter_context(nc.Block())

        @block.sync
        def _(sp):

            def mixer_unit(u):
                if u >= MIX_RING:
                    sp.wait_ge(s_lo, u - MIX_RING + 1)
                dst = ring[:, u % MIX_RING, :]
                if u < WIN_UNITS:
                    k = 4 * (u % 2)
                    sp.dma_start(dst.rearrange("p (k n) -> p k n", k=4), w_in[:, k:k + 4, BLOCKS[u // 2], :]).then_inc(s_raw[u % MIX_RING], 16)
                else:
                    k = 2 * (u - WIN_UNITS)
                    sp.dma_start(dst.rearrange("p (k n) -> p k n", k=2), w_o[:, k:k + 2, :]).then_inc(s_raw[u % MIX_RING], 16)

            mixer_unit(0)
            sp.dma_start(ident, t["c_main"][:, C_ID:C_ID + P]).then_inc(s_ident, 16)
            sp.dma_start(x_tok, t["x"].rearrange("(i p) d -> p i d", p=P)).then_inc(s_x, 16)
            mixer_unit(1)
            sp.dma_start(cst[:, P:NC], t["c_main"][:, P:NC]).then_inc(s_const, 16)
            mixer_unit(2)
            with nc.allow_non_contiguous_dma(reason="a few small parameters"):
                sp.dma_start(lb2, t["hgrn_lb_logits"].rearrange("r (a p) -> p r a", p=P)).then_inc(s_lb, 16)
            sp.dma_start(tab[0:N_BUCKETS, :], t["t5_bias"]).then_inc(s_tab, 16)
            sp.dma_start(rbias[:, 0:NG], t["b_group"].broadcast_to((P, NG))).then_inc(s_small, 16)
            sp.dma_start(rbias[:, NG:NL], t["b_expert"].broadcast_to((P, NE))).then_inc(s_small, 16)
            sp.dma_start(hot, t["c_hot"]).then_inc(s_tab, 16)
            sp.dma_start(nw[:, :], t["hgrn_norm_w"].broadcast_to((P, WIDTH))).then_inc(s_small, 16)
            for u in range(3, 6):
                mixer_unit(u)
            sp.wait_ge(s_stripsb, 2)
            sp.dma_start(strip_dram, strip_sb).then_inc(s_stripd, 16)
            for u in range(6, 14):
                mixer_unit(u)
            sp.wait_ge(s_av, T)
            sp.wait_ge(s_stripd, 16)
            for h in range(HEADS):
                skew = bass.AP(tensor=strip_dram.tensor, offset=h * STRIP, ap=[[1, P], [1, SEQ]])
                sp.dma_start(strips[:, h, :], skew).then_inc(s_strips, 16)
            for u in range(14, MIX_UNITS):
                mixer_unit(u)

            def expert_unit(m, e_g, e_d, slot):
                kind, half = m
                src, e = {"g": (wg, e_g), "u": (wu, e_g), "d": (wd, e_d)}[kind]
                sp.dma_start(ring[:, slot, :], src[bass.ds(e, 1), :, half * UNIT:(half + 1) * UNIT].rearrange("a p n -> (a p) n")).then_inc(s_raw[slot], 16)

            sp.wait_ge(s_mixtlo, KD)
            sp.dma_start(x_res, t["x"].rearrange("(i p) d -> p i d", p=P)).then_inc(s_xres, 16)
            sp.dma_start(lng, t["ln1_g"].broadcast_to((P, D))).then_inc(s_lnw, 16)
            sp.dma_start(lnb, t["ln1_b"].broadcast_to((P, D))).then_inc(s_lnw, 16)
            sp.dma_start(wr[:, :, 0:NG], t["w_group"].rearrange("(p k) g -> p k g", p=P)).then_inc(s_wr, 16)
            for g in range(NG):
                sp.dma_start(wr[:, :, NG + EPG * g:NG + EPG * (g + 1)],
                             t["w_expert"][g].rearrange("(p k) e -> p k e", p=P)).then_inc(s_wr, 16)
            order = [("g", 0), ("g", 1), ("u", 0), ("u", 1)]
            step = [("g", 0), ("g", 1), ("d", 0), ("d", 1), ("u", 0), ("u", 1)]
            for n, m in enumerate(order + step[:2]):
                expert_unit(m, n // 4, 0, (n + 3) % RING)
            for i in range(T):
                if i < T - 1:
                    sp.wait_ge(s_x1, i + 1)
                else:
                    sp.wait_ge(s_x1last, 1)
                sp.dma_start(x1_dram[i * P:(i + 1) * P, :], x_res[:, i, :]).then_inc(s_x1out, 16)
            sp.wait_ge(s_x1out, 16 * T)
            sp.wait_ge(s_x1t, T)
            for n in (6, 7, 8):
                expert_unit(step[n - 4], 1, 0, n + 3)
            sp.wait_ge(s_lo, 16)
            expert_unit(step[5], 1, 0, 0)
            for n in (10, 11):
                sp.wait_ge(s_lo, n + 7)
                expert_unit(step[n - 10], 2, 1, (n + 3) % RING)
            with sp.Fori(0, NE // 2 - 2) as j:
                for q in range(12):
                    n = 12 + q
                    sp.wait_ge(s_lo, n + 7 + 12 * j)
                    kind = step[(n - 4) % 6]
                    s = 1 + (n - 4) // 6
                    expert_unit(kind, s + 2 * j, s - 1 + 2 * j, (n + 3) % RING)
            for n in range(12 + 12 * (NE // 2 - 2), 6 * NE):
                s = 1 + (n - 4) // 6
                kind = step[(n - 4) % 6]
                if s == NE:
                    kind = [("d", 0), ("d", 1)][n - (4 + 6 * (NE - 1))]
                sp.wait_ge(s_lo, n + 7)
                expert_unit(kind, s, s - 1, (n + 3) % RING)

            sp.wait_ge(s_lo, MIX_UNITS + 6 * NE - RING + 3)
            sp.dma_start(f_x1, x1_dram.rearrange("(i p) d -> p i d", p=P)).then_inc(s_xo, 16)
            sp.dma_start(f_g, t["ln2_g"].broadcast_to((P, D))).then_inc(s_fw, 16)
            sp.dma_start(f_b, t["ln2_b"].broadcast_to((P, D))).then_inc(s_fw, 16)

            sp.wait_ge(s_flag, 2)
            over = sp.value_load(over_i[0:1, 0:1], min_val=0, max_val=1)
            with sp.If(over > 0):
                for b in range(2):
                    sp.wait_ge(s_yout[b], 16 * (NE // 2))
                ov_slots = slot_dram.rearrange("(r p e) c -> r e p c", p=P, e=NE)
                with sp.Fori(0, ROUNDS) as r:
                    with sp.Fori(0, NE) as e:
                        sp.wait_ge(s_ov["free"], r * NE + e + 1)
                        sp.dma_start(ov_rec[:, :], ov_slots[bass.ds(r + 1, 1), bass.ds(e, 1), :, :].rearrange("a b p c -> (a b p) c")).then_inc(s_ov["idx"], 16)
                        for q in range(6):
                            sp.dma_start(ring[:, OV_SLOTS[q], :], (wg, wu, wd)[q // 2][bass.ds(e, 1), :, (q % 2) * UNIT:(q % 2 + 1) * UNIT].rearrange("a p n -> (a p) n")).then_inc(s_ov["w"], 16)
                sp.wait_ge(s_ov["yout"], 16 * ROUNDS * NE)

            sp.wait_ge(s_lo, MIX_UNITS + 6 * NE)
            for b in range(2):
                sp.wait_ge(s_yout[b], 16 * (NE // 2))
            for i in range(T):
                for k in range(2):
                    sp.dma_start(f_pair(i)[:, k * D:(k + 1) * D],
                                 pair_dram[i * 2 * P:(i + 1) * 2 * P, :].rearrange("(p k) d -> p k d", k=2)[:, k, :]).then_inc(s_pairs[2 * i + k], 16)
            for i in range(T - 1):
                sp.wait_ge(s_fin, i + 1)
                sp.dma_start(out[i * P:(i + 1) * P, :], f_x1[:, i, :]).then_inc(s_out, 16)
            for half in range(2):
                sp.wait_ge(s_finlast, half + 1)
                cols = slice(half * D // 2, (half + 1) * D // 2)
                sp.dma_start(out[(T - 1) * P:, cols], f_x1[:, T - 1, cols]).then_inc(s_out, 16)
            sp.wait_ge(s_out, 16 * (T + 1))

        @block.gpsimd
        def _(pool):
            pool.wait_ge(s_small, 16 * 3)
            pool.wait_ge(s_scan, PAIRS)
            b_ch = hb.rearrange("p a (c s) -> p (a c) s", s=CH)
            pool.tensor_tensor(wlev[1].rearrange("p a (c s) -> p (a c) s", s=CH), b_ch,
                               b_ch[:, :, CH - 1:CH].broadcast_to((P, PAIRS * NCH, CH)), ALU.subtract).then_inc(s_d, 1)
            for l, m in enumerate(LEVELS):
                if l == 1:
                    pool.wait_ge(s_ket, T)
                elif l == 2:
                    pool.wait_ge(s_kv, NCH - 1)
                elif l == 3:
                    pool.wait_ge(s_inter, NCH)
                elif l >= 4:
                    pool.wait_ge(s_prod, 4 * (l - 4) + 8)
                src = hb.rearrange("p a (n s) -> p (a n) s", s=2 * m)
                pool.tensor_tensor(wlev[l].rearrange("p a (n s) -> p (a n) s", s=2 * m), src,
                                   src[:, :, m - 1:m].broadcast_to((P, SEQ * PAIRS // (2 * m), 2 * m)),
                                   ALU.subtract).then_inc(s_d, 1)
                if l == 1:
                    pool.wait_ge(s_evac, 4)
                    for i in range(T):
                        pool.tensor_tensor(gate[:, i, :], gate[:, i, :], nw[:, :], ALU.mult).then_inc(s_gate, 1)
            pool.wait_ge(s_const, 16)
            pool.tensor_copy(pad_i[:, :, :].rearrange("p e r -> p (e r)"), cst[:, C_PAD:C_PAD + 2 * NE]).then_inc(s_pool, 1)
            pool.tensor_copy(rec_i[:, :, :, :].rearrange("p i k r -> p (i k r)"), cst[:, C_PAIR:C_PAIR + 4 * T]).then_inc(s_pool, 1)
            pool.wait_ge(s_pool, 2)
            for r in range(SEQ // P):
                pool.dma_start(slot_dram[r * P * NE:(r + 1) * P * NE, :].rearrange("(p e) r -> p e r", e=NE),
                               pad_i[:, :, :]).then_inc(s_pads, 16)
            for i in range(T - 1):
                pool.wait_ge(s_lg, i + 1)
                pool.tensor_tensor(x_res[:, i, :], x_res[:, i, :], lnb, ALU.add).then_inc(s_x1, 1)
            pool.wait_ge(s_pads, 16 * (SEQ // P))
            pool.wait_ge(s_addr, 1)
            for i in range(T):
                for k in range(2):
                    pool.indirect_dma_start(out=slot_dram, out_offset=bass.IndirectOffsetOnAxis(ap=addr_i[:, i, k:k + 1].bitcast(U32), axis=0),
                                            in_=rec_i[:, i, k, :], in_offset=None).then_inc(s_slotw, 16)
            pool.wait_ge(s_slotw, 16 * 2 * T)
            pool.dma_start(slots[:, :, :], slot_dram[0:CAP * NE, :].rearrange("(p e) r -> p e r", e=NE)).then_inc(s_slots, 16)
            pool.wait_ge(s_slots, 16)
            pool.wait_ge(s_x1out, 16 * T)

            def gather(e):
                if e >= 2:
                    pool.wait_ge(s_et, e - 1)
                pool.indirect_dma_start(out=xg[:, e % 2, :], out_offset=None, in_=x1_dram,
                                        in_offset=bass.IndirectOffsetOnAxis(ap=slots[:, e, 0:1].bitcast(U32), axis=0)).then_inc(s_xg[e % 2], 16)

            gather(0)
            gather(1)
            for e in range(NE):
                if e + 2 < NE:
                    gather(e + 2)
                pool.wait_ge(s_y, e + 1)
                pool.indirect_dma_start(out=pair_dram, out_offset=bass.IndirectOffsetOnAxis(ap=slots[:, e, 1:2].bitcast(U32), axis=0),
                                        in_=yb[:, e % 2, :], in_offset=None, bounds_check=2 * SEQ - 1, oob_is_err=False).then_inc(s_yout[e % 2], 16)
            for b in range(2):
                pool.wait_ge(s_yout[b], 16 * (NE // 2))

            pool.wait_ge(s_flag, 2)
            over = pool.value_load(over_i[0:1, 0:1], min_val=0, max_val=1)
            with pool.If(over > 0):
                pool.sem_inc(s_ov["free"], 1)
                with pool.Fori(0, ROUNDS * NE) as i:
                    pool.wait_ge(s_ov["idx"], 16 * i + 16)
                    pool.sem_inc(s_ov["turn"], 1)
                    pool.indirect_dma_start(out=xg[:, 0, :], out_offset=None, in_=x1_dram,
                                            in_offset=bass.IndirectOffsetOnAxis(ap=ov_rec[:, 0:1].bitcast(U32), axis=0)).then_inc(s_ov["xg"], 16)
                    pool.wait_ge(s_ov["ysb"], i + 1)
                    pool.sem_inc(s_ov["turn"], 1)
                    pool.indirect_dma_start(out=pair_dram, out_offset=bass.IndirectOffsetOnAxis(ap=ov_rec[:, 1:2].bitcast(U32), axis=0),
                                            in_=yb[:, 0, :], in_offset=None, bounds_check=2 * SEQ - 1, oob_is_err=False).then_inc(s_ov["yout"], 16)
                    pool.wait_ge(s_ov["yout"], 16 * i + 16)
                    pool.sem_inc(s_ov["free"], 1)

            for i in range(T - 1):
                pool.wait_ge(s_fm, i + 1)
                pool.tensor_tensor(f_x1[:, i, :], f_x1[:, i, :], f_b, ALU.add).then_inc(s_fin, 1)

        @block.tensor
        def _(pe):
            def three(dst, lh, ll, rh, rl, first, last, done=None):
                pe.matmul(dst, lh, rh, start=first, stop=False, skip_group_check=True)
                pe.matmul(dst, lh, rl, start=False, stop=False, skip_group_check=True)
                return pe.matmul(dst, ll, rh, start=False, stop=last, skip_group_check=True)

            pe.wait_ge(s_x, 16)
            pe.wait_ge(s_ident, 16)
            for k in range(KD):
                for i in range(T):
                    last = pe.transpose(psum[:, k, i * P:(i + 1) * P], x_tok[:, i, k::KD], ident)
                last.then_inc(s_xt, 1)

            def project(n):
                base = 4 * (n % 2)
                by_channel = BLOCKS[n] in (0, 1, 3, 4)
                for u in (2 * n, 2 * n + 1):
                    pe.wait_ge(s_lo, u + 1)
                    w = u % WBUF
                    for kk in range(4):
                        k = 4 * (u % 2) + kk
                        if n == 0:
                            pe.wait_ge(s_xtlo, max(k + 1, 4))
                        for j in range(4):
                            ws = slice(kk * WIDTH + j * P, kk * WIDTH + (j + 1) * P)
                            wr_ = slice(kk * WIDTH, (kk + 1) * WIDTH)
                            ts = slice(j * P, (j + 1) * P)
                            first, last = k == 0, k == KD - 1
                            if by_channel:
                                ins = three(bank(base + j), w_hi[:, w, ws], w_lo[:, w, ws], act_hi[:, k, :], act_lo[:, k, :], first, last)
                            else:
                                ins = three(bank(base + j), act_hi[:, k, ts], act_lo[:, k, ts], w_hi[:, w, wr_], w_lo[:, w, wr_], first, last)
                    ins.then_inc(s_used, 1)

            for n in range(4):
                if n == 1:
                    pe.wait_ge(s_xtlo, KD)
                if n >= 2:
                    pe.wait_ge(s_evac, n - 1)
                if n == 1:
                    pe.wait_ge(s_tab, 32)
                    pe.wait_ge(s_flag, 1)
                    pe.matmul(psum[0:HEADS, 7, 0:512], tab, hot[:, 0:512], start=True, stop=True).then_inc(s_strip, 1)
                    pe.matmul(psum[0:HEADS, 6, 0:P], tab, hot[:, 512:STRIP], start=True, stop=True).then_inc(s_strip, 1)
                    pe.wait_ge(s_stripsb, 2)
                project(n)

            pe.wait_ge(s_ke, 1)
            pe.wait_ge(s_evac, 3)
            for i in range(T):
                if i >= 2:
                    pe.wait_ge(s_ketok, i - 1)
                for a in range(PAIRS):
                    last = pe.transpose(psum[:, 2 + i % 2, a * P:(a + 1) * P], wlev[1][:, a, i * P:(i + 1) * P], ident)
                last.then_inc(s_ket, 1)

            def diagonal(q):
                pg, par = q // 2, q % 2
                rows = slice(64 * par, 64 * par + 64)
                if q >= 2:
                    pe.wait_ge(s_copied, q - 1)
                for hh2 in range(2):
                    a = 2 * pg + hh2
                    for c in range(NCH):
                        cs = slice(c * CH, (c + 1) * CH)
                        o = psum[64 * (c % 2):64 * (c % 2) + 64, q % 2, hh2 * 256 + (c // 2) * CH:hh2 * 256 + (c // 2 + 1) * CH]
                        last = pe.matmul(o, hk[rows, a, cs], hq[rows, a, cs], start=(hh2 == 0 and c < 2), stop=True, skip_group_check=True)
                last.then_inc(s_prod, 1)

            def products(g):
                lev, a = g // 4 - 1, g % 4
                pe.wait_ge(s_copied, g - 1)
                pe.wait_ge(s_w, lev + 1)
                pe.wait_ge(s_qz, 8 * lev + 2 * a + 2)
                for c in range(NCH):
                    o = psum[64 * (c % 2):64 * (c % 2) + 64, g % 2, (c // 2) * CH:(c // 2 + 1) * CH]
                    last = pe.matmul(o, wlev[lev][:, a, c * CH:(c + 1) * CH], qz[:, a, c, :, :].rearrange("p h t -> p (h t)"),
                                     start=(c < 2), stop=True, skip_group_check=True)
                last.then_inc(s_prod, 1)

            pe.wait_ge(s_evac, 4)
            pe.wait_ge(s_qe, 1)
            pe.wait_ge(s_zero, 1)
            for c in range(NCH):
                rows = slice(64 * (c % 2), 64 * (c % 2) + 64)
                if c < NCH - 1:
                    if c == 0:
                        pe.wait_ge(s_ketok, T)
                    if c >= 2:
                        pe.wait_ge(s_state, c - 1)
                    for h in range(HEADS):
                        out_rows, hs = slice(64 * (h % 2), 64 * (h % 2) + 64), slice(h * DH, (h + 1) * DH)
                        last = pe.matmul(psum[out_rows, 2 + c % 2, hs], ke_tok[rows, c // 2, hs], hv[rows, c // 2, hs],
                                         start=(h < 2), stop=True, skip_group_check=True)
                    last.then_inc(s_kv, 1)
                if c < 4:
                    diagonal(c)
                else:
                    products(c)
                if c >= 1:
                    pe.wait_ge(s_state, c)
                for a in range(PAIRS):
                    last = pe.matmul(psum[rows, 4 + c // 2, a * P:(a + 1) * P], qe[:, a, c * CH:(c + 1) * CH],
                                     state[:, c % 2, a, :], start=(a == 0), stop=False, skip_group_check=True)
                last.then_inc(s_inter, 1)
            for g in range(8, GROUPS):
                products(g)
            pe.wait_ge(s_copied, GROUPS)
            for i in range(T):
                for h in range(HEADS):
                    a, par = h // 2, h % 2
                    for c in range(2):
                        rows = slice(64 * c, 64 * c + 64)
                        at = (a % 2) * 256 + i * CH
                        last = pe.matmul(psum[rows, 4 + i, h * DH:(h + 1) * DH], amat[rows, 2 * (a // 2) + par, at:at + CH],
                                         hv[rows, i, h * DH:(h + 1) * DH], start=False, stop=(h == HEADS - 1), skip_group_check=True)
                last.then_inc(s_av, 1)

            pe.wait_ge(s_copied, GROUPS)
            project(4)
            pe.wait_ge(s_r, T)
            project(5)
            pe.wait_ge(s_evac, 5)
            project(6)
            pe.wait_ge(s_evac, 6)
            def scores(n):
                h, i = unit(n)
                if n >= 2:
                    pe.wait_ge(s_logit, n)
                if i == 0:
                    pe.wait_ge(s_qklo, PAIRS + h // 2 + 1)
                qs, ks = slice(i * P, (i + 1) * P), slice(0, P * (i + 1))
                passes = [(aq_hi, ak_hi), (aq_hi, ak_lo), (aq_lo, ak_hi)]
                for m, (q, k) in enumerate(passes):
                    for par in range(2):
                        rows = slice(64 * par, 64 * par + 64)
                        last = pe.matmul(psum[:, 4 + par, ks], q[rows, h // 2, qs], k[rows, h // 2, ks], start=(m == 0), stop=(m == 2),
                                         skip_group_check=True)
                        if m == 2:
                            last.then_inc(s_score, 1)

            def probs_t(n):
                h, i = unit(n)
                pe.wait_ge(s_prob, n + 1)
                if n >= 2:
                    pe.wait_ge(s_ptsb, n - 1)
                for j in range(i + 1):
                    last = pe.transpose(psum[:, 6 + n % 2, j * P:(j + 1) * P], p_buf(h, i)[:, j * P:(j + 1) * P], ident)
                last.then_inc(s_pt, 1)

            def values(n):
                h, i = unit(n)
                pe.wait_ge(s_ptsb, n + 1)
                for j in range(i + 1):
                    last = pe.matmul(psum[:, i, h * DH:(h + 1) * DH], pt_buf(h, i)[:, j * P:(j + 1) * P], av[:, j, h * DH:(h + 1) * DH],
                                     start=(j == 0), stop=(j == i), skip_group_check=True)
                last.then_inc(s_pv, 1)

            for n in range(0, NU + 4, 2):
                if n < NU:
                    scores(n)
                for n2 in (n - 4, n - 3):
                    if 0 <= n2 < NU:
                        values(n2)
                for n2 in (n - 2, n - 1):
                    if 0 <= n2 < NU:
                        probs_t(n2)
            for n in range(KD):
                k = (4 + n) % KD
                src = mix_r if k >= 4 else mix_a
                if n >= 4:
                    pe.wait_ge(s_mixtlo, n - 3)
                else:
                    pe.wait_ge(s_mixr, T)
                    pe.wait_ge(s_ptsb, NU)
                if n == 4:
                    pe.wait_ge(s_mixa, T)
                for i in range(T):
                    last = pe.transpose(psum[:, 4 + n % 4, i * P:(i + 1) * P], src[:, i, (k % 4) * P:(k % 4 + 1) * P], ident)
                last.then_inc(s_mixt, 1)
            pe.wait_ge(s_mixtlo, KD)
            for q in range(WO_UNITS):
                u = WIN_UNITS + q
                pe.wait_ge(s_lo, u + 1)
                w = u % WBUF
                for i in range(T):
                    ts = slice(i * P, (i + 1) * P)
                    for half in range(2):
                        for kk in range(2):
                            k = 2 * q + kk
                            ws = slice(kk * D + half * 512, kk * D + half * 512 + 512)
                            ins = three(bank(2 * i + half), act_hi[:, k, ts], act_lo[:, k, ts], w_hi[:, w, ws], w_lo[:, w, ws],
                                        k == 0, k == KD - 1)
                    if q == WO_UNITS - 1 and i < T - 1:
                        ins.then_inc(s_wo, 1)
                ins.then_inc(s_used, 1)
            pe.wait_ge(s_wr, 16 * 5)
            for i in range(T + 1):
                if i < T:
                    if i < T - 1:
                        pe.wait_ge(s_x1, i + 1)
                    else:
                        pe.wait_ge(s_x1last, 1)
                    for k in range(KD):
                        last = pe.transpose(psum[:, 2 * i + k // 4, (k % 4) * P:(k % 4 + 1) * P], x_res[:, i, k::KD], ident)
                    last.then_inc(s_x1t, 1)
                if i >= 1:
                    pe.wait_ge(s_x1tsb, i)
                    for k in range(KD):
                        last = pe.matmul(psum[:, 2 * i - 2, 0:NL], x1t[:, (i - 1) % 2, k, :], wr[:, k, :], start=(k == 0), stop=(k == KD - 1))
                    last.then_inc(s_logits, 1)
            msk = rt[:, 0:T * NE].rearrange("p (i e) -> p i e", i=T)
            pe.wait_ge(s_mask, 1)
            flat_msk = msk.rearrange("p i e -> p (i e)")
            for gap in range(1, T + 1):
                last = pe.matmul(psum[:, 7, gap * NE:(T + 1) * NE], ones, flat_msk[:, 0:(T + 1 - gap) * NE], start=(gap == 1), stop=False,
                                 skip_group_check=True)
            last = pe.matmul(psum[:, 7, 0:T * NE], tri, flat_msk, start=False, stop=True, skip_group_check=True)
            last.then_inc(s_pos, 1)
            def transpose_x(e, b):
                pe.wait_ge(s_xg[b], 8 * (e - b) + 16)
                if not (isinstance(e, int) and e == 0):
                    pe.wait_ge(s_etlo, e)
                for k in range(KD):
                    last = pe.transpose(psum[:, k // 4, (k % 4) * P:(k % 4 + 1) * P], xg[:, b, k::KD], ident)
                last.then_inc(s_et, 1)

            def in_unit(dst, b, half, v0, j):
                pe.wait_ge(s_lo, MIX_UNITS + v0 + 1 + 12 * j)
                w = v0 % WBUF
                for kk in range(4):
                    k = 4 * half + kk
                    xs = slice(k * P, (k + 1) * P)
                    ws = slice(kk * DE, (kk + 1) * DE)
                    last = three(bank(dst), e_hi[:, b, xs], e_lo[:, b, xs], w_hi[:, w, ws], w_lo[:, w, ws], k == 0, k == KD - 1)
                last.then_inc(s_used, 1)

            def transpose_h(s):
                pe.wait_ge(s_h, s)
                for c in range(4):
                    last = pe.transpose(psum[:, 4, c * P:(c + 1) * P], hh[:, c::4], ident)
                last.then_inc(s_ht, 1)

            def down_unit(half, v0, j):
                pe.wait_ge(s_lo, MIX_UNITS + v0 + 1 + 12 * j)
                w = v0 % WBUF
                for cc in range(2):
                    c = 2 * half + cc
                    hs = slice(c * P, (c + 1) * P)
                    for dhalf in range(2):
                        ws = slice(cc * D + dhalf * 512, cc * D + dhalf * 512 + 512)
                        last = three(bank(5 + dhalf), h_hi[:, hs], h_lo[:, hs], w_hi[:, w, ws], w_lo[:, w, ws], c == 0, c == 3)
                last.then_inc(s_used, 1)

            def step(s0, j, following=True):
                s, b, v = s0 + 2 * j, s0 % 2, 4 + 6 * (s0 - 1)
                pe.wait_ge(s_etlo, s + 1)
                pe.wait_ge(s_silu, s)
                in_unit(2, b, 0, v, j)
                transpose_h(s)
                in_unit(2, b, 1, v + 1, j)
                pe.wait_ge(s_htlo, s)
                if s0 > 1:
                    pe.wait_ge(s_y, s - 1)
                down_unit(0, v + 2, j)
                down_unit(1, v + 3, j)
                if following:
                    transpose_x(s + 1, 1 - b)
                in_unit(3, b, 0, v + 4, j)
                in_unit(3, b, 1, v + 5, j)

            transpose_x(0, 0)
            pe.wait_ge(s_etlo, 1)
            in_unit(2, 0, 0, 0, 0)
            in_unit(2, 0, 1, 1, 0)
            transpose_x(1, 1)
            in_unit(3, 0, 0, 2, 0)
            in_unit(3, 0, 1, 3, 0)
            step(1, 0)
            with pe.Fori(0, NE // 2 - 2) as j:
                step(2, j)
                step(3, j)
            step(NE - 2, 0)
            step(NE - 1, 0, following=False)
            transpose_h(NE)
            pe.wait_ge(s_htlo, NE)
            pe.wait_ge(s_y, NE - 1)
            down_unit(0, 6 * NE - 2, 0)
            down_unit(1, 6 * NE - 1, 0)

            pe.wait_ge(s_flag, 2)
            over = pe.value_load(over_i[0:1, 0:1], min_val=0, max_val=1)
            with pe.If(over > 0):
                pe.wait_ge(s_y, NE)
                with pe.Fori(0, ROUNDS * NE) as i:
                    pe.wait_ge(s_ov["xg"], 16 * i + 16)
                    for k in range(KD):
                        last = pe.transpose(psum[:, k // 4, (k % 4) * P:(k % 4 + 1) * P], xg[:, 0, k::KD], ident)
                    last.then_inc(s_ov["xt"], 1)
                    pe.wait_ge(s_ov["xtsb"], i + 1)
                    pe.wait_ge(s_ov["w"], 16 * 6 * i + 16 * 6)
                    for which in range(2):
                        for k in range(KD):
                            last = pe.matmul(bank(2 + which), flat(6)[:, k * P:(k + 1) * P],
                                             ring[:, OV_SLOTS[2 * which + k // 4], (k % 4) * DE:(k % 4 + 1) * DE], start=(k == 0), stop=(k == KD - 1))
                    last.then_inc(s_ov["gu"], 1)
                    pe.wait_ge(s_ov["h"], i + 1)
                    for c in range(4):
                        last = pe.transpose(psum[:, 4, c * P:(c + 1) * P], hh[:, c::4], ident)
                    last.then_inc(s_ov["ht"], 1)
                    pe.wait_ge(s_ov["htsb"], i + 1)
                    for dhalf in range(2):
                        for c in range(4):
                            last = pe.matmul(bank(5 + dhalf), flat(7)[:, c * P:(c + 1) * P],
                                             ring[:, OV_SLOTS[4 + c // 2], (c % 2) * D + dhalf * 512:(c % 2) * D + dhalf * 512 + 512],
                                             start=(c == 0), stop=(c == 3))
                    last.then_inc(s_ov["y"], 1)

        @block.scalar
        def _(act):
            def hi(u):
                act.wait_ge(s_raw[u % MIX_RING], 16 * (u // MIX_RING) + 16)
                if u >= WBUF:
                    act.wait_ge(s_used, u - WBUF + 1)
                act.activation(w_hi[:, u % WBUF, :], ring[:, u % MIX_RING, :], ACT.Copy).then_inc(s_hi, 1)

            hi(0)
            for k in range(KD):
                act.wait_ge(s_xt, k + 1)
                act.activation(act_hi[:, k, :], bank(k), ACT.Copy).then_inc(s_xthi, 1)
            hi(1)
            act.wait_ge(s_lbready, 1)
            act.activation(lbe, lbe, ACT.Exp).then_inc(s_lnf, 1)
            for u in range(2, 4):
                hi(u)
            for half in range(2):
                act.wait_ge(s_strip, half + 1)
                n = 512 if half == 0 else P
                act.activation(strip_sb[:, 512 * half:512 * half + n], psum[0:HEADS, 7 - half, 0:n], ACT.Copy, scale=-1.0).then_inc(s_stripsb, 1)
            act.wait_ge(s_used, 2)
            act.activation(flat(8), banks(0, 4), ACT.Sigmoid).then_inc(s_evac, 1)
            hi(4)
            act.wait_ge(s_evac, 1)
            act.wait_ge(s_lbready, 2)
            for a in range(PAIRS):
                act.activation(logf[:, a, :], qe[:, a, :], ACT.Ln, scale=oml[:, a:a + 1], bias=lb[:, a:a + 1]).then_inc(s_lnf, 1)
            hi(5)
            act.wait_ge(s_used, 4)
            act.activation(flat(3), banks(4, 4), ACT.Silu).then_inc(s_evac, 1)
            hi(6)
            act.wait_ge(s_kk, PAIRS)
            act.wait_ge(s_scan, PAIRS)
            act.activation(flat(8), flat(5), ACT.Exp).then_inc(s_eb, 1)
            act.activation(flast, hb[:, :, CH - 1::CH], ACT.Exp).then_inc(s_eb, 1)
            act.wait_ge(s_d, 1)
            act.activation(flat(6), flat(6), ACT.Exp, scale=-1.0).then_inc(s_ed, 1)
            hi(7)
            act.wait_ge(s_used, 6)
            act.activation(flat(11), banks(0, 4), ACT.Copy).then_inc(s_evac, 1)
            hi(8)

            def level(l):
                m = LEVELS[l]
                act.wait_ge(s_d, l + 2)
                v = flat(LEVEL_SLOTS[l]).rearrange("p (n s) -> p n s", s=2 * m)
                act.activation(v[:, :, 0:m], v[:, :, 0:m], ACT.Exp, scale=-1.0).then_inc(s_ed, 1)
                act.activation(v[:, :, m:2 * m], v[:, :, m:2 * m], ACT.Exp).then_inc(s_ed, 1)

            level(0)
            hi(9)
            act.wait_ge(s_used, 8)
            act.activation(misc[:, 1024:3072], banks(4, 4), ACT.Sigmoid).then_inc(s_evac, 1)
            hi(10)
            act.wait_ge(s_scan, PAIRS)
            for i in range(T):
                act.wait_ge(s_ket, i + 1)
                act.activation(ke_tok[:, i, :], bank(2 + i % 2), ACT.Copy).then_inc(s_ketok, 1)
            for l in range(1, len(LEVELS)):
                level(l)
            for i in range(T):
                act.wait_ge(s_av, i + 1)
                if i >= 1:
                    act.wait_ge(s_ms, i)
                act.activation(sq[:, 0:512], bank(4 + i), ACT.Square).then_inc(s_sq, 1)
            act.wait_ge(s_ms, T + 1)
            act.activation(rs, ms, ACT.Sqrt).then_inc(s_sqrt, 1)
            hi(11)
            act.wait_ge(s_used, 10)
            act.activation(aq.rearrange("p a (i q) -> p (a i) q", q=P), turned(banks(0, 4)), ACT.Copy, scale=-SCALE).then_inc(s_evac, 1)
            hi(12)
            hi(13)
            act.wait_ge(s_used, 12)
            act.activation(flat(7), banks(4, 4), ACT.Copy).then_inc(s_evac, 1)
            hi(14)
            hi(15)
            act.wait_ge(s_used, 14)
            for a in range(PAIRS):
                act.activation(ak_hi[:, a, :], bank(a), ACT.Copy).then_inc(s_qkhi, 1)

            def q_hi(a):
                act.activation(aq_hi[:, a, :], aq[:, a, :], ACT.Copy).then_inc(s_qkhi, 1)

            q_hi(0)

            def probs(n):
                h, i = unit(n)
                act.wait_ge(s_logit, n + 1)
                col = h * T + i
                act.activation(p_buf(h, i), p_buf(h, i), ACT.Exp, scale=-1.0, bias=nmax[:, col:col + 1], accum_out=psums[:, col:col + 1]).then_inc(s_prob, 1)

            def pt_copy(n):
                h, i = unit(n)
                act.wait_ge(s_pt, n + 1)
                if h >= 2:
                    act.wait_ge(s_pv, n - 2 * T + 1)
                act.activation(pt_buf(h, i), psum[:, 6 + n % 2, 0:P * (i + 1)], ACT.Copy).then_inc(s_ptsb, 1)

            for n in range(0, NU + 2, 2):
                if n < NU:
                    probs(n)
                    probs(n + 1)
                if n >= 2:
                    pt_copy(n - 2)
                    pt_copy(n - 1)
                if n < 2 * (PAIRS - 1):
                    q_hi(n // 2 + 1)
                if n == 2 * PAIRS:
                    hi(16)
            for n in range(KD):
                k = (4 + n) % KD
                act.wait_ge(s_mixt, n + 1)
                src = bank(4 + n % 4).rearrange("p (i q) -> p i q", q=P) if k >= 4 else turned(bank(4 + n % 4))
                act.activation(act_hi[:, k, :].rearrange("p (i q) -> p i q", q=P), src, ACT.Copy).then_inc(s_mixthi, 1)
            hi(17)

            def ehi(v0, j):
                slot = (v0 + 3) % RING
                before = 1 + v0 // RING + (MIX_UNITS // MIX_RING if slot < MIX_RING else 0)
                act.wait_ge(s_raw[slot], 16 * before + 16 * j)
                act.wait_ge(s_used, MIX_UNITS + v0 - WBUF + 1 + 12 * j)
                act.activation(w_hi[:, v0 % WBUF, :], ring[:, slot, :], ACT.Copy).then_inc(s_hi, 1)

            ehi(0, 0)
            ehi(1, 0)
            act.wait_ge(s_eps, 2)
            def x1t_copy(i):
                act.wait_ge(s_x1t, i + 1)
                if i >= 2:
                    act.wait_ge(s_logits, i - 1)
                act.activation(misc[:, (i % 2) * D:(i % 2) * D + D], banks(2 * i, 2), ACT.Copy).then_inc(s_x1tsb, 1)

            for i in range(T):
                act.wait_ge(s_var, i + 1)
                act.activation(rstd[:, i:i + 1], mv[:, i, 1:2], ACT.Sqrt, bias=eps_ln).then_inc(s_std, 1)
                if i < T - 1:
                    act.wait_ge(s_ln, i + 1)
                    act.activation(x_res[:, i, :], x_res[:, i, :], ACT.Identity, scale=rstd[:, i:i + 1], bias=nmr[:, i:i + 1]).then_inc(s_x1n, 1)
                if i >= 1:
                    x1t_copy(i - 1)
            x1t_copy(T - 1)
            ehi(2, 0)
            act.wait_ge(s_rneed, 1)
            act.activation(r_ge, r_ge, ACT.Exp).then_inc(s_rexp, 1)
            act.wait_ge(s_rneed, 2)
            act.activation(r_ee, r_ee, ACT.Exp).then_inc(s_rexp, 1)

            def xt_hi(e, b):
                act.wait_ge(s_et, e + 1)
                act.activation(e_hi[:, b, :], banks(0, 2), ACT.Copy).then_inc(s_ethi, 1)

            def silu(e, v0, j):
                act.wait_ge(s_used, MIX_UNITS + v0 + 12 * j)
                act.activation(gs, bank(2), ACT.Silu).then_inc(s_silu, 1)

            def ht_hi(s):
                act.wait_ge(s_ht, s)
                act.activation(h_hi, bank(4), ACT.Copy).then_inc(s_hthi, 1)

            def y_out(e, b, v0, j):
                act.wait_ge(s_used, MIX_UNITS + v0 + 12 * j)
                if not (isinstance(e, int) and e < 2):
                    act.wait_ge(s_yout[b], 8 * (e - b))
                act.activation(yb[:, b, :], banks(5, 2), ACT.Copy).then_inc(s_y, 1)

            def step(s0, j, following=True, ahead=True):
                s, b, v = s0 + 2 * j, s0 % 2, 4 + 6 * (s0 - 1)
                ht_hi(s)
                ehi(v + 3, j)
                ehi(v + 4, j)
                silu(s, v + 2, j)
                ehi(v + 5, j)
                y_out(s - 1, 1 - b, v + 4, j)
                if following:
                    xt_hi(s + 1, 1 - b)
                ehi(v + 6, j)
                ehi(v + 7, j)
                if ahead:
                    ehi(v + 8, j)

            xt_hi(0, 0)
            ehi(3, 0)
            ehi(4, 0)
            silu(0, 2, 0)
            xt_hi(1, 1)
            ehi(5, 0)
            ehi(6, 0)
            step(1, 0)
            with act.Fori(0, NE // 2 - 2) as j:
                step(2, j)
                step(3, j)
            step(NE - 2, 0)
            step(NE - 1, 0, following=False, ahead=False)
            ht_hi(NE)
            act.wait_ge(s_xo, 16)
            act.activation(f_x1[:, :, :], f_x1[:, :, :], ACT.Copy, scale=ALPHA).then_inc(s_ft, 1)
            y_out(NE - 1, 1, 6 * NE, 0)

            act.wait_ge(s_flag, 2)
            over = act.value_load(over_i[0:1, 0:1], min_val=0, max_val=1)
            with act.If(over > 0):
                act.wait_ge(s_yout[0], 16 * (NE // 2))
                with act.Fori(0, ROUNDS * NE) as i:
                    act.wait_ge(s_ov["xt"], i + 1)
                    act.activation(flat(6)[:, 0:D], banks(0, 2), ACT.Copy).then_inc(s_ov["xtsb"], 1)
                    act.wait_ge(s_ov["gu"], i + 1)
                    act.activation(gs, bank(2), ACT.Silu).then_inc(s_ov["silu"], 1)
                    act.wait_ge(s_ov["ht"], i + 1)
                    act.activation(flat(7)[:, 0:512], bank(4), ACT.Copy).then_inc(s_ov["htsb"], 1)
                    act.wait_ge(s_ov["y"], i + 1)
                    act.activation(yb[:, 0, :], banks(5, 2), ACT.Copy).then_inc(s_ov["ysb"], 1)

            for i in range(T):
                act.wait_ge(s_fv, i + 1)
                act.activation(rstd[:, i:i + 1], mv[:, i, 1:2], ACT.Sqrt, bias=eps_ln).then_inc(s_fs, 1)
                if i == T - 1:
                    continue
                act.wait_ge(s_fl, i + 1)
                act.activation(f_x1[:, i, :], f_x1[:, i, :], ACT.Identity, scale=rstd[:, i:i + 1], bias=nmr[:, i:i + 1]).then_inc(s_fn, 1)

        @block.vector
        def _(dve):
            links = [0]

            def link(ins):
                links[0] += 1
                ins.then_inc(s_dve, 1)
                dve.wait_ge(s_dve, links[0])

            def lo(u):
                dve.wait_ge(s_hi, u + 1)
                if u >= WBUF:
                    dve.wait_ge(s_used, u - WBUF + 1)
                dve.tensor_tensor(w_lo[:, u % WBUF, :], ring[:, u % MIX_RING, :], w_hi[:, u % WBUF, :].bitcast(F32), ALU.subtract).then_inc(s_lo, 1)

            dve.memset(tab[N_BUCKETS:N_BUCKETS + 1, :], -BIG).then_inc(s_flag, 1)
            dve.memset(eps_ln, LN_EPS).then_inc(s_eps, 1)
            dve.memset(eps_rms, RMS_EPS).then_inc(s_eps, 1)
            lo(0)
            for k in range(KD):
                dve.wait_ge(s_xthi, k + 1)
                dve.tensor_tensor(act_lo[:, k, :], bank(k), act_hi[:, k, :].bitcast(F32), ALU.subtract).then_inc(s_xtlo, 1)
            dve.wait_ge(s_lb, 16)
            link(dve.tensor_tensor(lbm, lb2[:, 0, :], lb2[:, 1, :], ALU.max))
            dve.tensor_tensor(lbe[:, 0, :], lb2[:, 0, :], lbm, ALU.subtract)
            dve.tensor_tensor(lbe[:, 1, :], lb2[:, 1, :], lbm, ALU.subtract).then_inc(s_lbready, 1)
            lo(1)
            dve.wait_ge(s_lnf, 1)
            link(dve.tensor_tensor(lbs, lbe[:, 0, :], lbe[:, 1, :], ALU.add))
            link(dve.reciprocal(lbs, lbs))
            link(dve.tensor_tensor(lb, lbe[:, 0, :], lbs, ALU.mult))
            link(dve.tensor_scalar(lb, lb, F_FLOOR, None, ALU.max))
            link(dve.tensor_scalar(oml, lb, -1.0, 1.0, ALU.mult, ALU.add))
            dve.tensor_scalar(noml, oml, -1.0, None, ALU.mult).then_inc(s_lbready, 1)
            lo(2)
            lo(3)
            lo(4)
            dve.wait_ge(s_evac, 1)
            dve.wait_ge(s_lbready, 2)
            for a in range(PAIRS):
                dve.tensor_scalar(hk[:, a, :], qe[:, a, :], noml[:, a:a + 1], oml[:, a:a + 1], ALU.mult, ALU.add).then_inc(s_kk, 1)
            for a in range(PAIRS):
                dve.wait_ge(s_lnf, a + 2)
                dve.tensor_tensor_scan(hb[:, a, :], cst[:, C_SCAN:C_SCAN + SEQ], logf[:, a, :], 0.0, ALU.mult, ALU.add).then_inc(s_scan, 1)
            lo(5)
            lo(6)
            dve.wait_ge(s_evac, 2)
            dve.wait_ge(s_eb, 1)
            dve.tensor_tensor(flat(8), flat(8), flat(3), ALU.mult).then_inc(s_qe, 1)
            dve.wait_ge(s_ed, 1)
            dve.wait_ge(s_kk, PAIRS)
            dve.tensor_tensor(flat(6), flat(6), flat(4), ALU.mult).then_inc(s_ke, 1)
            lo(7)
            dve.memset(misc[:, 0:1024], 0.0).then_inc(s_zero, 1)
            dve.memset(flat(10), 0.0).then_inc(s_memz, 1)
            lo(8)

            def decayed_keys(l):
                m = LEVELS[l]
                dve.wait_ge(s_ed, 2 * l + 2)
                view = lambda f: f.rearrange("p (n s) -> p n s", s=2 * m)
                v, k = view(flat(LEVEL_SLOTS[l])), view(flat(4))
                dve.tensor_tensor(v[:, :, 0:m], v[:, :, 0:m], k[:, :, 0:m], ALU.mult).then_inc(s_w, 1)

            def decayed_queries(l, a):
                m = LEVELS[l]
                if l > 0:
                    dve.wait_ge(s_prod, 4 * l + a + 1)
                dve.wait_ge(s_ed, 2 * l + 3)
                for par in range(2):
                    rows = slice(64 * par, 64 * par + 64)
                    right = lambda f: f[rows, a, :].rearrange("p (c n s) -> p c n s", c=NCH, s=2 * m)[:, :, :, m:2 * m]
                    dve.tensor_tensor(qz[rows, a, :, par, :].rearrange("p c (n t) -> p c n t", t=m), right(wlev[l]), right(hq), ALU.mult).then_inc(s_qz, 1)

            def keep(g):
                dve.wait_ge(s_prod, g + 1)
                if g == 0:
                    dve.wait_ge(s_memz, 1)
                mask = cst[:, C_MASK + 64 * (g // 4):C_MASK + 64 * (g // 4) + 64].bitcast(U32)
                if g < 4:
                    dst = amat[:, g, :].rearrange("p (n t) -> p n t", t=CH)
                    dve.copy_predicated(dst, mask.rearrange("p (a t) -> p a t", a=1).broadcast_to((P, 8, CH)),
                                        bank(g % 2).rearrange("p (n t) -> p n t", t=CH)).then_inc(s_copied, 1)
                    return
                dve.wait_ge(s_copied, max(g - 3, 4))
                a, m = g % 4, LEVELS[g // 4 - 1]
                mask = mask.rearrange("p (a b t) -> p a b t", a=1, t=2 * m)[:, :, :, m:2 * m].broadcast_to((P, T, CH // (2 * m), m))
                for par in range(2):
                    dst = amat[:, 2 * (a // 2) + par, (a % 2) * 256:(a % 2) * 256 + 256].rearrange("p (i n s) -> p i n s", i=T, s=2 * m)[:, :, :, m:2 * m]
                    src = bank(g % 2, 256).rearrange("p (i h n t) -> p i h n t", i=T, h=2, t=m)[:, :, par, :, :]
                    ins = dve.copy_predicated(dst, mask, src)
                    ins.then_inc(s_copied if par else s_half, 1)

            dve.wait_ge(s_stripd, 16)
            dve.memset(misc[:, 3072:5120], 0.0).then_inc(s_zero, 1)
            decayed_keys(0)
            dve.wait_ge(s_zero, 2)
            for a in range(PAIRS):
                decayed_queries(0, a)
            lo(9)
            lo(10)
            dve.wait_ge(s_eb, 2)
            dve.wait_ge(s_zero, 1)
            for c in range(NCH):
                keep(c)
                if c == 3:
                    decayed_keys(1)
                if c >= 4:
                    decayed_queries(1, c - 4)
                if c < NCH - 1:
                    dve.wait_ge(s_kv, c + 1)
                    if c >= 1:
                        dve.wait_ge(s_inter, c)
                    for hh2 in range(2):
                        rows = slice(64 * hh2, 64 * hh2 + 64)
                        now, nxt = state[rows, c % 2, :, rows], state[rows, (c + 1) % 2, :, rows]
                        dec = flast[rows, :, c:c + 1].broadcast_to((64, PAIRS, 64))
                        dve.tensor_tensor(nxt, now, dec, ALU.mult).then_inc(s_st1, 1)
                    for hh2 in range(2):
                        rows = slice(64 * hh2, 64 * hh2 + 64)
                        nxt = state[rows, (c + 1) % 2, :, rows]
                        kv = bank(2 + c % 2).rearrange("p (a v) -> p a v", a=PAIRS)[rows, :, rows]
                        dve.wait_ge(s_st1, 2 * c + 1 + hh2)
                        ins = dve.tensor_tensor(nxt, nxt, kv, ALU.add)
                        if hh2 == 0:
                            ins.then_inc(s_st2, 1)
                    ins.then_inc(s_state, 1)
                    dve.wait_ge(s_state, c + 1)
                    dve.wait_ge(s_st2, c + 1)
            for g in range(8, GROUPS):
                keep(g)
                if g // 4 < len(LEVELS):
                    if g % 4 == 0:
                        decayed_keys(g // 4)
                    decayed_queries(g // 4, g % 4)
            for i in range(T):
                dve.wait_ge(s_sq, i + 1)
                dve.tensor_reduce(ms[:, 8 * i:8 * i + 8], sq[:, 0:512].rearrange("p (h v) -> p h v", v=DH), AX.X, ALU.add).then_inc(s_ms, 1)
            dve.wait_ge(s_ms, T)
            dve.tensor_scalar(ms, ms, 1.0 / DH, RMS_EPS, ALU.mult, ALU.add).then_inc(s_ms, 1)
            dve.wait_ge(s_sqrt, 1)
            link(dve.reciprocal(rs, rs))
            for i in range(T):
                scale = rs[:, 8 * i:8 * i + 8].rearrange("p (h a) -> p h a", a=1).broadcast_to((P, HEADS, DH))
                dve.tensor_tensor(mix_r[:, i, :].rearrange("p (h v) -> p h v", v=DH), bank(4 + i).rearrange("p (h v) -> p h v", v=DH),
                                  scale, ALU.mult).then_inc(s_r, 1)
            dve.wait_ge(s_gate, T)
            for i in range(T):
                dve.wait_ge(s_r, i + 1)
                dve.tensor_tensor(mix_r[:, i, :], mix_r[:, i, :], gate[:, i, :], ALU.mult).then_inc(s_mixr, 1)
            lo(11)
            for u in range(12, 16):
                lo(u)
            for a in range(PAIRS):
                dve.wait_ge(s_qkhi, a + 1)
                dve.tensor_tensor(ak_lo[:, a, :], bank(a), ak_hi[:, a, :].bitcast(F32), ALU.subtract).then_inc(s_qklo, 1)

            def q_lo(a):
                dve.wait_ge(s_qkhi, PAIRS + a + 1)
                dve.tensor_tensor(aq_lo[:, a, :], aq[:, a, :], aq_hi[:, a, :].bitcast(F32), ALU.subtract).then_inc(s_qklo, 1)

            q_lo(0)
            dve.wait_ge(s_strips, 16 * HEADS)
            for n in range(NU):
                h, i = unit(n)
                if n % 2 == 0 and 2 <= n < 2 * PAIRS:
                    q_lo(n // 2)
                if n == 2 * PAIRS + 2:
                    lo(16)
                dve.wait_ge(s_score, n + 1)
                if h >= 2:
                    dve.wait_ge(s_pt, n - 2 * T + 1)
                w = P * (i + 1)
                dve.tensor_tensor_reduce(p_buf(h, i), psum[:, 4 + n % 2, 0:w], strips[:, h, SEQ - w:SEQ], 1.0, 3.0e38,
                                         ALU.add, ALU.min, nmax[:, h * T + i:h * T + i + 1]).then_inc(s_logit, 1)
            dve.wait_ge(s_prob, NU)
            link(dve.reciprocal(prec, psums))
            for i in range(T):
                dve.wait_ge(s_pv, NU - 2 * T + 2 * i + 2)
                scale = prec.rearrange("p (h i a) -> p i h a", i=T, a=1)[:, i, :, :].broadcast_to((P, HEADS, DH))
                dve.tensor_tensor(mix_a[:, i, :].rearrange("p (h v) -> p h v", v=DH), bank(i).rearrange("p (h v) -> p h v", v=DH),
                                  scale, ALU.mult).then_inc(s_mixa, 1)
            for n in range(KD):
                k = (4 + n) % KD
                dve.wait_ge(s_mixthi, n + 1)
                src = bank(4 + n % 4).rearrange("p (i q) -> p i q", q=P) if k >= 4 else turned(bank(4 + n % 4))
                dve.tensor_tensor(act_lo[:, k, :].rearrange("p (i q) -> p i q", q=P), src,
                                  act_hi[:, k, :].bitcast(F32).rearrange("p (i q) -> p i q", q=P), ALU.subtract).then_inc(s_mixtlo, 1)
            lo(17)

            def elo(v0, j):
                slot = (v0 + 3) % RING
                dve.wait_ge(s_hi, MIX_UNITS + v0 + 1 + 12 * j)
                dve.wait_ge(s_used, MIX_UNITS + v0 - WBUF + 1 + 12 * j)
                dve.tensor_tensor(w_lo[:, v0 % WBUF, :], ring[:, slot, :], w_hi[:, v0 % WBUF, :].bitcast(F32), ALU.subtract).then_inc(s_lo, 1)

            elo(0, 0)
            elo(1, 0)
            dve.wait_ge(s_xres, 16)
            dve.wait_ge(s_lnw, 32)

            def shift_scale(i):
                link(dve.reciprocal(rstd[:, i:i + 1], rstd[:, i:i + 1]))
                return dve.scalar_tensor_tensor(out=nmr[:, i:i + 1], in0=mv[:, i, 0:1], scalar=-1.0, in1=rstd[:, i:i + 1], op0=ALU.mult, op1=ALU.mult)

            def norm_tail(x, i, g, b, ready, std, pieces=1):
                dve.scalar_tensor_tensor(out=x, in0=x, scalar=mv[:, i, 0:1], in1=g, op0=ALU.subtract, op1=ALU.mult).then_inc(s_cent, 1)
                dve.wait_ge(std, i + 1)
                link(dve.reciprocal(rstd[:, i:i + 1], rstd[:, i:i + 1]))
                dve.wait_ge(s_cent, 1 if ready is s_x1last else 2)
                w = D // pieces
                for q in range(pieces):
                    xs = slice(q * w, (q + 1) * w)
                    dve.scalar_tensor_tensor(out=x[:, xs], in0=x[:, xs], scalar=rstd[:, i:i + 1], in1=b[:, xs], op0=ALU.mult, op1=ALU.add).then_inc(ready, 1)

            def stats(x, i):
                for half in range(2):
                    dve.bn_stats(bst[:, i, half, :], x[:, 512 * half:512 * half + 512]).then_inc(s_bn, 1)

            def routed(i):
                dve.wait_ge(s_logits, i + 1)
                dve.tensor_tensor(r_l[:, i, :], psum[:, 2 * i, 0:NL], rbias, ALU.add).then_inc(s_lin, 1)

            dve.wait_ge(s_small, 48)
            for i in range(T + 1):
                if i < T:
                    if i < T - 1:
                        dve.wait_ge(s_wo, i + 1)
                    else:
                        dve.wait_ge(s_used, MIX_UNITS)
                    for half in range(2):
                        xs = x_res[:, i, 512 * half:512 * half + 512]
                        dve.scalar_tensor_tensor(out=xs, in0=xs, scalar=ALPHA, in1=bank(2 * i + half), op0=ALU.mult, op1=ALU.add).then_inc(s_res, 1)
                if 1 <= i < T:
                    dve.wait_ge(s_std, i)
                    shift_scale(i - 1).then_inc(s_ln, 1)
                if i < T:
                    dve.wait_ge(s_res, 2 * i + 2)
                    stats(x_res[:, i, :], i)
                    dve.wait_ge(s_bn, 2 * i + 2)
                    dve.bn_aggr(mv[:, i, :], bst[:, i, :, :].rearrange("p b n -> p (b n)")).then_inc(s_var, 1)
                    dve.wait_ge(s_var, i + 1)
                if 1 <= i < T:
                    dve.wait_ge(s_x1n, i)
                    dve.tensor_tensor(x_res[:, i - 1, :], x_res[:, i - 1, :], lng, ALU.mult).then_inc(s_lg, 1)
                if i == T:
                    norm_tail(x_res[:, T - 1, :], T - 1, lng, lnb, s_x1last, s_std)
                if i >= 2:
                    routed(i - 2)
            elo(2, 0)
            routed(T - 1)

            def bc(ap, n):
                return ap.broadcast_to((P, T, n))

            dve.wait_ge(s_lin, T)
            gl = r_l[:, :, 0:NG]
            link(dve.tensor_reduce(r_m, gl, AX.X, ALU.max))
            dve.tensor_tensor(r_g, gl, bc(r_m, NG), ALU.subtract).then_inc(s_rneed, 1)
            dve.wait_ge(s_rexp, 1)
            w4 = cst[:, C_W4:C_W4 + 4].rearrange("p (a n) -> p a n", a=1)

            def first_max(e, hot, top):
                link(dve.tensor_reduce(top, e, AX.X, ALU.max))
                link(dve.tensor_tensor(hot, e, bc(top, 4), ALU.is_equal))
                link(dve.tensor_tensor(hot, hot, bc(w4, 4), ALU.mult))
                link(dve.tensor_reduce(r_m, hot, AX.X, ALU.max))
                link(dve.tensor_tensor(hot, hot, bc(r_m, 4), ALU.is_equal))

            link(dve.tensor_reduce(r_gsum, r_g, AX.X, ALU.add))
            link(dve.reciprocal(r_gw, r_gsum))
            first_max(r_g, r_gh, r_top)
            in_group = r_gh.rearrange("p t (g a) -> p t g a", a=1).broadcast_to((P, T, NG, EPG))
            r_sel0 = r_sel[:, 0].rearrange("p t (g e) -> p t g e", g=NG)
            link(dve.tensor_tensor(r_sel0, r_l[:, :, NG:NL].rearrange("p t (g e) -> p t g e", g=NG), in_group, ALU.mult))
            link(dve.tensor_reduce(r_e, r_sel[:, 0].rearrange("p t (g e) -> p t e g", g=NG), AX.X, ALU.add))
            link(dve.tensor_reduce(r_m, r_e, AX.X, ALU.max))
            dve.tensor_tensor(r_e, r_e, bc(r_m, EPG), ALU.subtract).then_inc(s_rneed, 1)
            dve.wait_ge(s_rexp, 2)
            first_max(r_e, r_h[:, 0], r_top)
            link(dve.scalar_tensor_tensor(out=r_tmp, in0=r_h[:, 0], scalar=-2.0, in1=r_e, op0=ALU.mult, op1=ALU.add))
            first_max(r_tmp, r_h[:, 1], r_top2)
            for k in range(2):
                ins = dve.tensor_tensor(r_sel[:, k].rearrange("p t (g e) -> p t g e", g=NG),
                                        r_h[:, k].rearrange("p t (a e) -> p t a e", a=1).broadcast_to((P, T, NG, EPG)), in_group, ALU.mult)
                if k == 0:
                    ins.then_inc(s_sel, 1)
            link(ins)
            dve.wait_ge(s_sel, 1)
            dve.tensor_tensor(r_msk, r_sel[:, 0], r_sel[:, 1], ALU.add).then_inc(s_mask, 1)
            dve.wait_ge(s_pos, 1)
            pos = psum[:, 7, 0:T * NE].rearrange("p (i e) -> p i e", i=T)
            e16 = cst[:, C_E16:C_E16 + NE].rearrange("p (a e) -> p a e", a=1)
            link(dve.tensor_scalar(r_pos, pos, float(NE), None, ALU.mult))
            link(dve.tensor_tensor(r_pos, r_pos, bc(e16, NE), ALU.add))
            for k in range(2):
                link(dve.tensor_tensor(r_t16, r_pos, r_sel[:, k], ALU.mult))
                link(dve.tensor_reduce(r_adr[:, :, k:k + 1], r_t16, AX.X, ALU.add))
            dve.tensor_copy(addr_i[:, :, :], r_adr).then_inc(s_addr, 1)
            link(dve.tensor_tensor(r_gsum, r_top, r_top2, ALU.add))
            link(dve.reciprocal(r_gsum, r_gsum))
            link(dve.tensor_tensor(r_gw, r_gw, r_gsum, ALU.mult))
            link(dve.tensor_tensor(wgt[:, :, 0:1], r_gw, r_top, ALU.mult))
            link(dve.tensor_tensor(wgt[:, :, 1:2], r_gw, r_top2, ALU.mult))
            link(dve.tensor_reduce(r_cnt, psum[:, 7, T * NE:(T + 1) * NE], AX.X, ALU.max))
            link(dve.tensor_scalar(r_cnt, r_cnt, float(CAP), None, ALU.is_gt))
            dve.tensor_copy(over_i[:, :], r_cnt).then_inc(s_flag, 1)

            def xt_lo(e, b):
                dve.wait_ge(s_ethi, e + 1)
                dve.tensor_tensor(e_lo[:, b, :], banks(0, 2), e_hi[:, b, :].bitcast(F32), ALU.subtract).then_inc(s_etlo, 1)

            def hidden(e, v0, j):
                dve.wait_ge(s_used, MIX_UNITS + v0 + 12 * j)
                dve.wait_ge(s_silu, e + 1)
                dve.tensor_tensor(hh, bank(3), gs, ALU.mult).then_inc(s_h, 1)

            def step(s0, j, following=True, ahead=True):
                s, b, v = s0 + 2 * j, s0 % 2, 4 + 6 * (s0 - 1)
                dve.wait_ge(s_hthi, s)
                dve.tensor_tensor(h_lo, bank(4), h_hi.bitcast(F32), ALU.subtract).then_inc(s_htlo, 1)
                elo(v + 3, j)
                elo(v + 4, j)
                elo(v + 5, j)
                if following:
                    xt_lo(s + 1, 1 - b)
                elo(v + 6, j)
                elo(v + 7, j)
                hidden(s, v + 6, j)
                if ahead:
                    elo(v + 8, j)

            xt_lo(0, 0)
            elo(3, 0)
            elo(4, 0)
            xt_lo(1, 1)
            elo(5, 0)
            hidden(0, 4, 0)
            elo(6, 0)
            step(1, 0)
            with dve.Fori(0, NE // 2 - 2) as j:
                step(2, j)
                step(3, j)
            step(NE - 2, 0)
            step(NE - 1, 0, following=False, ahead=False)
            dve.wait_ge(s_hthi, NE)
            dve.tensor_tensor(h_lo, bank(4), h_hi.bitcast(F32), ALU.subtract).then_inc(s_htlo, 1)

            dve.wait_ge(s_flag, 2)
            over = dve.value_load(over_i[0:1, 0:1], min_val=0, max_val=1)
            with dve.If(over > 0):
                with dve.Fori(0, ROUNDS * NE) as i:
                    dve.wait_ge(s_ov["silu"], i + 1)
                    dve.tensor_tensor(hh, bank(3), gs, ALU.mult).then_inc(s_ov["h"], 1)

            dve.wait_ge(s_ft, 1)
            dve.wait_ge(s_fw, 32)
            for i in range(T + 1):
                if i < T:
                    dve.wait_ge(s_pairs[2 * i], 16)
                    y = f_x1[:, i, :]
                    dve.scalar_tensor_tensor(out=y, in0=f_pair(i)[:, 0:D], scalar=wgt[:, i, 0:1], in1=y, op0=ALU.mult, op1=ALU.add).then_inc(s_facc, 1)
                if 1 <= i < T:
                    dve.wait_ge(s_fs, i)
                    shift_scale(i - 1).then_inc(s_fl, 1)
                if i < T:
                    dve.wait_ge(s_pairs[2 * i + 1], 16)
                    dve.wait_ge(s_facc, 2 * i + 1)
                    dve.scalar_tensor_tensor(out=y, in0=f_pair(i)[:, D:2 * D], scalar=wgt[:, i, 1:2], in1=y, op0=ALU.mult, op1=ALU.add).then_inc(s_facc, 1)
                if 1 <= i < T:
                    dve.wait_ge(s_fn, i)
                    dve.tensor_tensor(f_x1[:, i - 1, :], f_x1[:, i - 1, :], f_g, ALU.mult).then_inc(s_fm, 1)
                if i < T:
                    dve.wait_ge(s_facc, 2 * i + 2)
                    stats(y, i)
                    dve.wait_ge(s_bn, 2 * (T + i) + 2)
                    dve.bn_aggr(mv[:, i, :], bst[:, i, :, :].rearrange("p b n -> p (b n)")).then_inc(s_fv, 1)
                    dve.wait_ge(s_fv, i + 1)
            norm_tail(f_x1[:, T - 1, :], T - 1, f_g, f_b, s_finlast, s_fs, 2)


SHAPES = {
    "x": (SEQ, D), "w_in": (D, 7 * WIDTH), "t5_bias": (N_BUCKETS, HEADS), "hgrn_lb_logits": (2, WIDTH), "hgrn_norm_w": (1, WIDTH),
    "w_o": (D, D), "ln1_g": (1, D), "ln1_b": (1, D), "w_group": (D, NG), "b_group": (1, NG), "w_expert": (NG, D, EPG),
    "b_expert": (1, NE), "w_gate": (NE, D, DE), "w_up": (NE, D, DE), "w_down": (NE, DE, D), "ln2_g": (1, D), "ln2_b": (1, D),
}


def kernel(**inputs):
    import concourse.bacc as bacc
    from concourse.bass_utils import run_bass_kernel_spmd as run

    nc = bacc.Bacc("TRN2", target_bir_lowering=False, num_devices=1)
    arrays, t = {}, {}
    main, hot = shape_constants()
    laid = {n: np.ascontiguousarray(inputs[n]).reshape(s) for n, s in SHAPES.items()}
    laid["c_main"], laid["c_hot"] = main, hot
    for n, a in laid.items():
        arrays["in_" + n] = a
        t[n] = nc.dram_tensor("in_" + n, a.shape, mybir.dt.from_np(a.dtype), kind="ExternalInput").ap()
    out = nc.dram_tensor("out", (SEQ, D), F32, kind="ExternalOutput").ap()
    build(nc, t, out)
    return run(nc, [arrays], core_ids=[0]).results[0]["out"].reshape(1, SEQ, D)
```
